# Optimizing a Trainium2 kernel written in Bass

```python
import math
import jax, jax.numpy as jnp
from jax import lax
import numpy as np

D_MODEL = 1024
BATCH = 1
SEQ = 256
DEPTH = 2
DEC_BATCH = 1
DEC_SEQ = 1024
PAST_LEN = 256

GRID_W = 64
N_HEADS = 16
HEAD_DIM = D_MODEL // N_HEADS
WIN_H = 8
WIN_W = 16
Q_BW = WIN_W
KEY_BW = 2 * WIN_W
CTX_QBLOCK = 128
D_FF = ((8 * D_MODEL // 3 + 255) // 256) * 256
N_BANDS = 16
PE_DIM = 1 + 2 * N_BANDS
FILT_W = 64
MOD_SHIFT = 0.05
DECAY_MIN = math.log(1e2) / 1.5
DECAY_MAX = math.log(1e2) / 0.3
N_HY = (DEPTH + 1) // 2
N_NA = DEPTH // 2
ALPHA = (2 * DEPTH) ** 0.25
BETA = (8 * DEPTH) ** -0.25
LN_EPS = 1e-5

kernel_name = "hyena_natten_deepnorm_dit_step"

def layer_norm(x, g, b):
    xf = x.astype(jnp.float32)
    mu = jnp.mean(xf, axis=-1, keepdims=True)
    var = jnp.mean(jnp.square(xf - mu), axis=-1, keepdims=True)
    return ((xf - mu) * lax.rsqrt(var + LN_EPS) * g + b).astype(x.dtype)

def ada_params(cvec, w, b):
    m = (jax.nn.silu(cvec) @ w + b)[:, None, :]
    return jnp.split(m, 6, axis=-1)

def centred_conv3(z, w, b):
    zp = jnp.pad(z, ((0, 0), (1, 1), (0, 0)))
    return zp[:, :-2] * w[0] + zp[:, 1:-1] * w[1] + zp[:, 2:] * w[2] + b

def hyena_filters(L, pe_w1, pe_b1, pe_w2, pe_b2, pe_w3, sin_freq, decay):
    t = jnp.linspace(0.0, 1.0, L, dtype=jnp.float32)[:, None]
    w = (2.0 * math.pi / L) * jnp.arange(L, dtype=jnp.float32)[:, None]
    bands = jnp.linspace(1e-4, N_BANDS - 1, N_BANDS, dtype=jnp.float32)[None, :]
    feats = jnp.concatenate([t, jnp.cos(bands * w), jnp.sin(bands * w)], axis=-1)
    hdn = jnp.sin(sin_freq[0] * (feats @ pe_w1 + pe_b1))
    hdn = jnp.sin(sin_freq[1] * (hdn @ pe_w2 + pe_b2))
    k = (hdn @ pe_w3).astype(jnp.float32) * (jnp.exp(-t * jnp.abs(decay)) + MOD_SHIFT)
    return k[:, :D_MODEL], k[:, D_MODEL:]

def bidir_long_conv(v, k_fwd, k_bwd, bias):
    L = v.shape[1]
    k_circ = jnp.concatenate([k_fwd, jnp.zeros((1, D_MODEL), jnp.float32), k_bwd[:0:-1]], axis=0)
    kf = jnp.fft.rfft(k_circ, axis=0)
    vf = jnp.fft.rfft(v.astype(jnp.float32), n=2 * L, axis=1)
    y = jnp.fft.irfft(vf * kf[None], n=2 * L, axis=1)[:, :L]
    return (y + v.astype(jnp.float32) * bias).astype(v.dtype)

def hyena_mixer(u, w_in, sconv_w, sconv_b, k_fwd, k_bwd, bias, w_out):
    z = centred_conv3(u @ w_in, sconv_w, sconv_b)
    x0, x1, v = jnp.split(z, 3, axis=-1)
    y = bidir_long_conv(v * x1, k_fwd, k_bwd, bias) * x0
    return y @ w_out

def split_heads(qkv):
    B, L, _ = qkv.shape
    qkv = qkv.reshape(B, L, 3, N_HEADS, HEAD_DIM).transpose(2, 0, 3, 1, 4)
    return qkv[0], qkv[1], qkv[2]

def merge_heads(o):
    B, H, L, d = o.shape
    return o.transpose(0, 2, 1, 3).reshape(B, L, H * d)

def na_context(h, w_qkv, w_out):
    B, S, _ = h.shape
    q, k, v = split_heads(h @ w_qkv)
    nb = S // CTX_QBLOCK
    qb = jnp.moveaxis(q.reshape(B, N_HEADS, nb, CTX_QBLOCK, HEAD_DIM), 2, 0) * HEAD_DIM ** -0.5

    def attend(qblk):
        s = jnp.einsum('bhqd,bhkd->bhqk', qblk, k).astype(jnp.float32)
        p = jax.nn.softmax(s, axis=-1).astype(v.dtype)
        return jnp.einsum('bhqk,bhkd->bhqd', p, v)

    o = jnp.moveaxis(lax.map(attend, qb), 0, 2).reshape(B, N_HEADS, S, HEAD_DIM)
    return merge_heads(o) @ w_out, k, v

def na_latent(h, k_ctx, v_ctx, w_qkv, rpb, w_out):
    B, L, _ = h.shape
    rows = L // GRID_W
    kh = min(WIN_H, rows)
    nj = GRID_W // Q_BW
    nk = kh * KEY_BW
    q, k, v = split_heads(h @ w_qkv)
    r = np.arange(rows)
    row0 = np.clip(r - kh // 2, 0, rows - kh)
    key_rows = row0[:, None] + np.arange(kh)[None, :]
    j = np.arange(nj)
    band0 = np.clip(j * Q_BW - WIN_W // 2, 0, GRID_W - KEY_BW)
    key_cols = band0[:, None] + np.arange(KEY_BW)[None, :]
    idx = (key_rows[:, None, :, None] * GRID_W + key_cols[None, :, None, :]).reshape(rows, nj, nk)
    kg = k[:, :, idx]
    vg = v[:, :, idx]
    qb = q.reshape(B, N_HEADS, rows, nj, Q_BW, HEAD_DIM) * HEAD_DIM ** -0.5
    q_cols = j[:, None] * Q_BW + np.arange(Q_BW)[None, :]
    win0 = np.clip(q_cols - WIN_W // 2, 0, GRID_W - WIN_W)
    kc = key_cols[:, None, :]
    col_ok = (kc >= win0[..., None]) & (kc < win0[..., None] + WIN_W)
    valid = np.broadcast_to(col_ok[:, :, None, :], (nj, Q_BW, kh, KEY_BW)).reshape(nj, Q_BW, nk)
    dr_i = (key_rows - r[:, None] + WIN_H - 1)[:, None, None, :, None]
    dc_i = np.clip(kc - q_cols[:, :, None] + WIN_W - 1, 0, 2 * WIN_W - 2)[None, :, :, None, :]
    bias = rpb[:, dr_i, dc_i].reshape(N_HEADS, rows, nj, Q_BW, nk).astype(jnp.float32)
    s_loc = jnp.einsum('bhrjqd,bhrjkd->bhrjqk', qb, kg).astype(jnp.float32) + bias[None]
    s_loc = jnp.where(valid, s_loc, -jnp.inf)
    s_ctx = jnp.einsum('bhrjqd,bhkd->bhrjqk', qb, k_ctx).astype(jnp.float32)
    p = jax.nn.softmax(jnp.concatenate([s_loc, s_ctx], axis=-1), axis=-1).astype(v.dtype)
    o = (jnp.einsum('bhrjqk,bhrjkd->bhrjqd', p[..., :nk], vg)
         + jnp.einsum('bhrjqk,bhkd->bhrjqd', p[..., nk:], v_ctx))
    o = o.reshape(B, N_HEADS, L, HEAD_DIM)
    return merge_heads(o) @ w_out

def swiglu(h, w_in, w_out):
    g, u = jnp.split(h @ w_in, 2, axis=-1)
    return (jax.nn.silu(g) * u) @ w_out

def setup_inputs(seed: int = 0) -> dict:
    key = jax.random.key(seed)
    ks = iter(jax.random.split(key, 40))
    f32 = jnp.float32

    def nrm(shape, scale):
        return jax.random.normal(next(ks), shape, f32) * scale

    D = D_MODEL
    return {
        "x_prompt": nrm((BATCH, SEQ, D), 1.0),
        "x_sample": nrm((DEC_BATCH, DEC_SEQ, D), 1.0),
        "cache_k": nrm((DEC_BATCH, N_NA, N_HEADS, PAST_LEN, HEAD_DIM), 1.0),
        "cache_v": nrm((DEC_BATCH, N_NA, N_HEADS, PAST_LEN, HEAD_DIM), 1.0),
        "c": nrm((DEC_BATCH, D), 1.0),
        "c_ctx": nrm((D,), 1.0),
        "ada_w": nrm((DEPTH, D, 6 * D), 0.5 * D ** -0.5),
        "ada_b": nrm((DEPTH, 6 * D), 0.02),
        "ln1_g": 1.0 + nrm((DEPTH, D), 0.02),
        "ln1_b": nrm((DEPTH, D), 0.02),
        "ln2_g": 1.0 + nrm((DEPTH, D), 0.02),
        "ln2_b": nrm((DEPTH, D), 0.02),
        "ffn_w_in": nrm((DEPTH, D, 2 * D_FF), D ** -0.5),
        "ffn_w_out": nrm((DEPTH, D_FF, D), BETA * D_FF ** -0.5),
        "hy_w_in": nrm((N_HY, D, 3 * D), D ** -0.5),
        "hy_sconv_w": nrm((N_HY, 3, 3 * D), 3 ** -0.5),
        "hy_sconv_b": nrm((N_HY, 3 * D), 0.02),
        "hy_pe_w1": nrm((N_HY, PE_DIM, FILT_W), PE_DIM ** -0.5),
        "hy_pe_b1": nrm((N_HY, FILT_W), 0.02),
        "hy_pe_w2": nrm((N_HY, FILT_W, FILT_W), FILT_W ** -0.5),
        "hy_pe_b2": nrm((N_HY, FILT_W), 0.02),
        "hy_pe_w3": nrm((N_HY, FILT_W, 2 * D), FILT_W ** -0.5),
        "hy_sin_freq": 1.0 + nrm((N_HY, 2, FILT_W), 0.1),
        "hy_decay": jax.random.uniform(next(ks), (N_HY, 2 * D), f32, DECAY_MIN, DECAY_MAX),
        "hy_bias": nrm((N_HY, D), 1.0),
        "hy_w_out": nrm((N_HY, D, D), BETA * D ** -0.5),
        "na_w_qkv": nrm((N_NA, D, 3 * D), D ** -0.5),
        "na_rpb": nrm((N_NA, N_HEADS, 2 * WIN_H - 1, 2 * WIN_W - 1), 0.1),
        "na_w_out": nrm((N_NA, D, D), BETA * D ** -0.5),
    }

def reference(x_prompt, x_sample, cache_k, cache_v, c, c_ctx, ada_w, ada_b, ln1_g, ln1_b, ln2_g, ln2_b,
              ffn_w_in, ffn_w_out, hy_w_in, hy_sconv_w, hy_sconv_b, hy_pe_w1, hy_pe_b1, hy_pe_w2, hy_pe_b2,
              hy_pe_w3, hy_sin_freq, hy_decay, hy_bias, hy_w_out, na_w_qkv, na_rpb, na_w_out):
    xp, xs = x_prompt, x_sample
    new_k, new_v = [], []
    for i in range(DEPTH):
        sh1_p, sc1_p, g1_p, sh2_p, sc2_p, g2_p = ada_params(c_ctx[None, :], ada_w[i], ada_b[i])
        sh1_s, sc1_s, g1_s, sh2_s, sc2_s, g2_s = ada_params(c, ada_w[i], ada_b[i])
        hp = xp * (1.0 + sc1_p) + sh1_p
        hs = xs * (1.0 + sc1_s) + sh1_s
        j = i // 2
        if i % 2 == 0:
            filt = (hy_pe_w1[j], hy_pe_b1[j], hy_pe_w2[j], hy_pe_b2[j], hy_pe_w3[j], hy_sin_freq[j], hy_decay[j])
            kf_p, kb_p = hyena_filters(xp.shape[1], *filt)
            kf_s, kb_s = hyena_filters(xs.shape[1], *filt)
            op = hyena_mixer(hp, hy_w_in[j], hy_sconv_w[j], hy_sconv_b[j], kf_p, kb_p, hy_bias[j], hy_w_out[j])
            os_ = hyena_mixer(hs, hy_w_in[j], hy_sconv_w[j], hy_sconv_b[j], kf_s, kb_s, hy_bias[j], hy_w_out[j])
        else:
            op, k_ctx, v_ctx = na_context(hp, na_w_qkv[j], na_w_out[j])
            new_k.append(k_ctx)
            new_v.append(v_ctx)
            os_ = na_latent(hs, cache_k[:, j], cache_v[:, j], na_w_qkv[j], na_rpb[j], na_w_out[j])
        xp = layer_norm(ALPHA * xp + g1_p * op, ln1_g[i], ln1_b[i])
        xs = layer_norm(ALPHA * xs + g1_s * os_, ln1_g[i], ln1_b[i])
        fp = swiglu(xp * (1.0 + sc2_p) + sh2_p, ffn_w_in[i], ffn_w_out[i])
        fs = swiglu(xs * (1.0 + sc2_s) + sh2_s, ffn_w_in[i], ffn_w_out[i])
        xp = layer_norm(ALPHA * xp + g2_p * fp, ln2_g[i], ln2_b[i])
        xs = layer_norm(ALPHA * xs + g2_s * fs, ln2_g[i], ln2_b[i])
    new_k_arr = jnp.stack(new_k, axis=1)
    new_v_arr = jnp.stack(new_v, axis=1)
    return (xp, xs, new_k_arr, new_v_arr)


_drawn_inputs = setup_inputs


def setup_inputs(seed=0):
    import zlib

    import numpy as np

    out = dict(_drawn_inputs(seed))
    spreads = {}
    factors = {'cache_k': 8.0, 'cache_v': 7.547, 'na_rpb': 64.0}
    for name, (base, spread) in spreads.items():
        noise = np.random.default_rng([zlib.crc32(name.encode()), seed]).standard_normal(out[name].shape)
        drawn = base * np.exp(spread * noise) if base else spread * noise
        out[name] = __import__('jax').numpy.asarray(drawn.astype(out[name].dtype))
    for name, factor in factors.items():
        out[name] = (out[name] * factor).astype(out[name].dtype)
    return out
```

```python
import concourse.bass as bass
from concourse import mybir
from contextlib import ExitStack
import math
import numpy as np

F32 = mybir.dt.float32
F32R = mybir.dt.float32r
BF16 = mybir.dt.bfloat16
ALU = mybir.AluOpType
ACT = mybir.ActivationFunctionType
AX = mybir.AxisListType

D = 1024
KT = D // 128
LS, LP = 1024, 256
TOK = LS + LP
CHUNKS = ((0, 512), (512, 1024), (1024, TOK))
PARTS = ((0, LS), (LS, TOK))
DFF = 2816
FC = DFF // 256
NH, HD = 16, 64
GW = 64
ALPHA = (2 * 2) ** 0.25
EPS = 1e-5
FILT, PE_DIM = 64, 33
TWO_PI_HI = 6.28125
TWO_PI_LO = 2 * math.pi - TWO_PI_HI
MAGIC = 12582912.0
MASKED = -1e30
RPB_H, RPB_W = 23, 63
BANDS = (0, 8, 24, 32)
BIAS_X = (16, 8, 8, 0)
BIAS_T = (0, 1, 1, 2)
SH1, SC1, G1, SH2, SC2, G2 = range(6)

E_FILT, E_IN, E_FWD, E_INV, E_OUT, E_FFN, E_QKV = 20, 24, 9, 24, 8, 6 * FC, 24


def hyena_natten_step(nc, t):
    ctx = ExitStack()
    with ctx:
        names = [0]

        def sb(name, shape, dt=F32, where=ctx):
            names[0] += 1
            return where.enter_context(nc.sbuf_tensor(f"{name}_{names[0]}", shape, dt))

        def sem(name, where=ctx):
            names[0] += 1
            if where is ctx:
                return ctx.enter_context(nc.semaphore(f"{name}_{names[0]}"))
            handle = nc.alloc_semaphore(f"{name}_{names[0]}")
            stage_sems.append(handle)
            return handle

        stage_sems = []

        def clear():
            nc.clear_and_free_semaphores(stage_sems)
            stage_sems.clear()
            nc.all_engine_barrier()

        def stage():
            st = ExitStack()
            st.callback(clear)
            return st


        raw = sb("w_raw", [128, 2, 1024])
        wh = sb("w_hi", [128, 2, 1024], F32R)
        wl = sb("w_lo", [128, 2, 1024], F32R)
        ident = sb("ident", [128, 128])
        meanw = sb("meanw", [128, 128])
        par = sb("par", [128, 264])
        conv_p = par[:, 0:96].rearrange("p (t n) -> p t n", n=4)
        ln_p = par[:, 96:160].rearrange("p (s k) -> p s k", k=8)
        hb_p = par[:, 160:168]
        adab = par[:, 168:264]
        mod = sb("mod", [128, 96, 2])
        silc = sb("silc", [128, 8, 2])
        aff = sb("aff", [128, 2, 8, 2])
        axs = sb("axs", [128, 2, 8])
        eps = sb("eps", [128, 1])
        a_h = sb("a_hi", [128, KT, TOK], F32R)
        a_l = sb("a_lo", [128, KT, TOK], F32R)

        def dram(name, shape):
            return nc.dram_tensor(name, shape, F32).ap()
        spec = dram("spec", (10, 128, 2, D))
        x0_d = dram("x0_d", (KT, 128, TOK))
        s_d = dram("s_d", (KT, 128, TOK))
        y_d = dram("y_d", (KT, 3, 128, 8, 128))
        qkv_d = dram("qkv_d", (24, 128, TOK))
        x_d = dram("x_d", (KT, 128, TOK))

        w_loaded = [sem("w_loaded0"), sem("w_loaded1")]
        w_hi, w_split, w_used = sem("w_hi"), sem("w_split"), sem("w_used")

        def at(c, i=None, n=0):
            return c if i is None or n == 0 else i * n + c

        def load_entry(sp, c, src, i=None, n=0, width=1024):
            if c >= 2:
                sp.wait_ge(w_split, at(c - 1, i, n))
            sp.dma_start(raw[:, c % 2, 0:width], src).then_inc(w_loaded[c % 2], 16)

        def split_hi(act, c, i=None, n=0, width=1024):
            s = c % 2
            act.wait_ge(w_loaded[s], at(16 * (c // 2) + 16, i, 8 * n))
            if c >= 2:
                act.wait_ge(w_used, at(c - 1, i, n))
            act.activation(wh[:, s, 0:width], raw[:, s, 0:width], ACT.Copy).then_inc(w_hi, 1)

        def split_lo(pool, c, i=None, n=0, width=1024):
            s = c % 2
            pool.wait_ge(w_hi, at(c + 1, i, n))
            pool.tensor_tensor(wl[:, s, 0:width], raw[:, s, 0:width], wh[:, s, 0:width].bitcast(F32),
                               ALU.subtract).then_inc(w_split, 1)

        def products(pe, c, blocks, chunks, start=True, stop=True):
            for b, (blk, xh, xl, out) in enumerate(blocks):
                for term, (w, x) in enumerate(((wh, xh), (wh, xl), (wl, xh))):
                    for c0, c1 in chunks:
                        last = pe.matmul(out[:, c0:c1], w[:, c % 2, blk * 128:blk * 128 + 128], x[:, c0:c1],
                                         start=start and b == 0 and term == 0,
                                         stop=stop and b == len(blocks) - 1 and term == 2)
            return last

        def wsrc(w):
            return t["w_all"][w, :, :]

        fst = ExitStack()
        hd2 = sb("hd2", [FILT, TOK], F32, fst)
        hdb = sb("hdb", [FILT, 2, 128], F32, fst)
        negt = sb("negt", [128, 10], F32, fst)
        with stage() as st:
            cvec = sb("cvec", [128, 8, 2], F32, st)
            awr = sb("ada_raw0", [128, 2, 1024], F32, st)
            feats = sb("feats", [PE_DIM, TOK], F32, st)
            w1 = sb("pe_w1", [PE_DIM, FILT], F32, st)
            w2 = sb("pe_w2", [FILT, FILT], F32, st)
            fcol = sb("fcol", [FILT, 4], F32, st)
            arg = sb("arg", [FILT, TOK], F32, st)
            cyc = sb("cyc", [FILT, TOK], F32, st)
            hd = sb("hd", [FILT, TOK], F32, st)
            ps_mlp = st.enter_context(nc.psum_tensor("ps_mlp", [128, 1536], F32))
            ps_ada = st.enter_context(nc.psum_tensor("ps_ada", [128, 512], F32))
            c_in, a_in, pe_a, sil_ok = sem("c_in", st), [sem("a_in0", st), sem("a_in1", st)], sem("pe_a", st), sem("sil_ok", st)
            mlp_mm, arg_ok, dve_s, hd_ok, clr = sem("mlp_mm", st), sem("arg_ok", st), sem("dve_s", st), sem("hd_ok", st), sem("clr", st)
            block = st.enter_context(nc.Block())

            @block.sync
            def _(sp):
                for dst, src in ((cvec[:, :, :], t["cvec"]), (par[:, :], t["par"]), (ident[:, :], t["ident"]),
                                 (feats[:, :], t["feats"]), (w1[:, :], t["pe_w1"]), (w2[:, :], t["pe_w2"]),
                                 (fcol[:, :], t["fcol"]), (negt[:, :], t["negt"])):
                    sp.dma_start(dst, src).then_inc(c_in, 16)
                load_entry(sp, 0, wsrc(0))
                load_entry(sp, 1, wsrc(1))

            @block.gpsimd
            def _(pool):
                pool.memset(meanw[:, :], 1.0 / D)
                pool.memset(eps[:, :], EPS)
                split_lo(pool, 0)
                split_lo(pool, 1)

            @block.scalar
            def _(act):
                for n in range(2):
                    act.dma_start(awr[:, n, :], t["ada"][n, :, :]).then_inc(a_in[n], 16)
                act.wait_ge(c_in, 128)
                act.activation(silc[:, :, :], cvec[:, :, :], ACT.Silu).then_inc(sil_ok, 1)
                split_hi(act, 0)
                split_hi(act, 1)
                with act.Fori(0, 7) as i:
                    for n in range(2):
                        act.wait_ge(pe_a, i * 2 + (n + 1))
                        act.dma_start(awr[:, n, :], t["ada"][i * 2 + (n + 2), :, :]).then_inc(a_in[n], 16)
                act.wait_ge(arg_ok, 1)
                act.activation(hd[:, :], arg[:, :], ACT.Sin).then_inc(hd_ok, 1)
                act.wait_ge(arg_ok, 2)
                act.activation(hd2[:, :], arg[:, :], ACT.Sin).then_inc(hd_ok, 1)
                act.wait_ge(hd_ok, 2)
                act.activation(hdb[:, 0, :], hd2[:, 0:128], ACT.Copy).then_inc(hd_ok, 1)
                act.activation(hdb[:, 1, :], hd2[:, LS:LS + 128], ACT.Copy).then_inc(hd_ok, 1)

            @block.vector
            def _(dve):
                dve.wait_ge(c_in, 128)
                for layer, (b, q) in enumerate(((0, 2), (1, 3))):
                    dve.wait_ge(mlp_mm, layer + 1)
                    dve.tensor_scalar(arg[:, :], ps_mlp[0:FILT, 0:TOK], fcol[:, b:b + 1],
                                      fcol[:, q:q + 1], ALU.add, ALU.mult).then_inc(dve_s, 1)
                    dve.wait_ge(dve_s, 5 * layer + 1)
                    dve.tensor_scalar(cyc[:, :], arg[:, :], 1.0 / (2 * math.pi), MAGIC, ALU.mult,
                                      ALU.add).then_inc(dve_s, 1)
                    dve.wait_ge(dve_s, 5 * layer + 2)
                    dve.tensor_scalar(cyc[:, :], cyc[:, :], MAGIC, None, ALU.subtract).then_inc(dve_s, 1)
                    dve.wait_ge(dve_s, 5 * layer + 3)
                    dve.scalar_tensor_tensor(arg[:, :], cyc[:, :], -TWO_PI_HI, arg[:, :], ALU.mult,
                                             ALU.add).then_inc(dve_s, 1)
                    dve.wait_ge(dve_s, 5 * layer + 4)
                    dve.scalar_tensor_tensor(arg[:, :], cyc[:, :], -TWO_PI_LO, arg[:, :], ALU.mult,
                                             ALU.add).then_inc(dve_s, 1)
                    dve.wait_ge(dve_s, 5 * layer + 5)
                    dve.tensor_scalar(arg[:, :], arg[:, :], 3.1415925, -3.1415925, ALU.min,
                                      ALU.max).then_inc(arg_ok, 1)
                dve.wait_ge(hd_ok, 4)
                dve.memset(hdb[:, :, 0:1], 0.0)
                dve.wait_ge(pe_a, 16)
                dve.tensor_tensor(mod[:, 0:16, :], ps_ada[:, 0:32].rearrange("p (a b) -> p a b", b=2),
                                  adab[:, 0:16].unsqueeze(2).to_broadcast([128, 16, 2]), ALU.add)

            @block.tensor
            def _(pe):
                pe.wait_ge(c_in, 128)
                for c0, c1 in CHUNKS:
                    last = pe.matmul(ps_mlp[0:FILT, c0:c1], w1[:, :], feats[:, c0:c1], start=True, stop=True)
                last.then_inc(mlp_mm, 1)
                pe.wait_ge(sil_ok, 1)
                with pe.Fori(0, 8) as i:
                    for n in range(2):
                        pe.wait_ge(a_in[n], i * 16 + 16)
                        for k in range(8):
                            last = pe.matmul(ps_ada[:, bass.ds(i * 4 + 2 * n, 2)], awr[:, n, k * 128:k * 128 + 128],
                                             silc[:, k, :], start=k == 0, stop=k == 7)
                        last.then_inc(pe_a, 1)
                pe.wait_ge(hd_ok, 1)
                for c0, c1 in CHUNKS:
                    last = pe.matmul(ps_mlp[0:FILT, c0:c1], w2[:, :], hd[:, c0:c1], start=True, stop=True)
                last.then_inc(mlp_mm, 1)

        e0 = 0
        with stage() as st:
            w3 = sb("pe_w3", [FILT, 2, 512], F32, st)
            dec = sb("dec", [128, 2, 512], F32, st)
            win = sb("win", [128, 2, 2, 512], F32, st)
            ker = sb("ker", [128, 2, 2, 512], F32, st)
            pq = sb("pq", [128, 2, 2, 512], F32, st)
            pqh = sb("pq_hi", [128, 10, 2, 512], F32R, st)
            pql = a_l[:, :, :].rearrange("p k t -> p (k t)")[:, 0:10240].rearrange("p (n s c) -> p n s c", n=10, s=2)
            odd = sb("odd", [128, 2, 512], F32, st)
            gout = sb("gout", [128, 2, 2, 512], F32, st)
            ps = [st.enter_context(nc.psum_tensor(f"ps_f{b}", [128, 512], F32)) for b in range(8)]
            f_w, dec_ok, pe_k, win_ok, ker_ok, pq_ok, ph_ok, pl_ok = [
                sem(n, st) for n in ("f_w", "dec_ok", "pe_k", "win_ok", "ker_ok", "pq_ok", "ph_ok", "pl_ok")]
            odd_ok, spec_ev, g_out = sem("odd_ok", st), sem("spec_ev", st), [sem("g_out0", st), sem("g_out1", st)]
            block = st.enter_context(nc.Block())

            @block.sync
            def _(sp):
                sp.sem_inc(g_out[0], 1)
                sp.sem_inc(g_out[1], 1)
                with sp.Fori(0, 2) as i:
                    for j in range(10):
                        load_entry(sp, e0 + 2 + j, wsrc(i * 10 + (e0 + 2 + j)), i, 10)
                        sp.wait_ge(spec_ev, 1 + i * 10 + (j + 1))
                        a = j // 2
                        for side, tile in enumerate((a, 4 + (a ^ 1)) if j < 8 else (8, 9)):
                            sp.dma_start(spec[tile, :, j % 2, bass.ds(i * 512, 512)],
                                         gout[:, j % 2, side, :]).then_inc(g_out[j % 2], 16)
                for s in range(2):
                    sp.wait_ge(g_out[s], 321)

            @block.gpsimd
            def _(pool):
                with pool.Fori(0, 2) as i:
                    for n in range(10):
                        pool.wait_ge(ph_ok, i * 10 + (n + 1))
                        pool.tensor_tensor(pql[:, n, :, :], pq[:, n % 2, :, :], pqh[:, n, :, :].bitcast(F32),
                                           ALU.subtract).then_inc(pl_ok, 1)
                    for j in range(10):
                        split_lo(pool, e0 + 2 + j, i, 10)

            @block.scalar
            def _(act):
                with act.Fori(0, 2) as i:
                    act.dma_start(dec[:, :, :], t["dec"][i, :, :, :]).then_inc(f_w, 16)
                    act.dma_start(w3[:, :, :], t["pe_w3"][i, :, :, :]).then_inc(f_w, 16)
                    act.wait_ge(f_w, i * 32 + 32)
                    act.activation(dec[:, :, :], dec[:, :, :], ACT.Abs).then_inc(dec_ok, 1)
                    act.wait_ge(dec_ok, i + 1)
                    for n in range(11):
                        if n < 10:
                            if n >= 2:
                                act.wait_ge(ker_ok, i * 10 + (n - 1))
                            act.activation(win[:, n % 2, :, :], dec[:, :, :], ACT.Exp,
                                           scale=negt[:, n:n + 1]).then_inc(win_ok, 1)
                        if n >= 1:
                            act.wait_ge(pq_ok, i * 10 + n)
                            act.activation(pqh[:, n - 1, :, :], pq[:, (n - 1) % 2, :, :],
                                           ACT.Copy).then_inc(ph_ok, 1)
                    for j in range(10):
                        act.wait_ge(w_used, i * 10 + (e0 + j + 1))
                        split_hi(act, e0 + 2 + j, i, 10)
                        if j >= 2:
                            act.wait_ge(spec_ev, 1 + i * 10 + (j - 1))
                        act.activation(odd[:, j % 2, :], ps[2 * (j % 4) + 1][:, :], ACT.Copy).then_inc(odd_ok, 1)

            @block.vector
            def _(dve):
                dve.sem_inc(spec_ev, 1)
                with dve.Fori(0, 2) as i:
                    for n in range(10):
                        dve.wait_ge(win_ok, i * 10 + (n + 1))
                        dve.wait_ge(pe_k, i * 10 + (n + 1))
                        for side in range(2):
                            ins = dve.scalar_tensor_tensor(ker[:, n % 2, side, :], win[:, n % 2, side, :], 0.05,
                                                           ps[2 * (n % 2) + side][:, :], ALU.add, ALU.mult)
                        ins.then_inc(ker_ok, 1)
                        dve.wait_ge(ker_ok, i * 10 + (n + 1))
                        if n >= 2:
                            dve.wait_ge(pl_ok, i * 10 + (n - 1))
                        dve.tensor_tensor(pq[:, n % 2, 0, :], ker[:, n % 2, 0, :], ker[:, n % 2, 1, :], ALU.add)
                        dve.tensor_tensor(pq[:, n % 2, 1, :], ker[:, n % 2, 0, :], ker[:, n % 2, 1, :],
                                          ALU.subtract).then_inc(pq_ok, 1)
                    for j in range(10):
                        dve.wait_ge(g_out[j % 2], 1 + i * 160 + 32 * (j // 2))
                        dve.wait_ge(odd_ok, i * 10 + (j + 1))
                        even = ps[2 * (j % 4)]
                        dve.tensor_tensor(gout[:, j % 2, 0, :], even[:, :], odd[:, j % 2, :], ALU.add)
                        if j % 2 == 0:
                            ins = dve.tensor_tensor(gout[:, j % 2, 1, :], even[:, :], odd[:, j % 2, :], ALU.subtract)
                        else:
                            ins = dve.scalar_tensor_tensor(gout[:, j % 2, 1, :], even[:, :], -1.0,
                                                           odd[:, j % 2, :], ALU.mult, ALU.add)
                        ins.then_inc(spec_ev, 1)

            @block.tensor
            def _(pe):
                with pe.Fori(0, 2) as i:
                    pe.wait_ge(spec_ev, 1 + i * 10)
                    pe.wait_ge(f_w, i * 32 + 32)
                    for n in range(10):
                        if n >= 2:
                            pe.wait_ge(ker_ok, i * 10 + (n - 1))
                        fwd = hd2[:, n * 128:n * 128 + 128]
                        bwd = hdb[:, n // 8, :] if n in (0, 8) else fwd
                        pe.matmul(ps[2 * (n % 2)][:, :], fwd, w3[:, 0, :], start=True, stop=True)
                        pe.matmul(ps[2 * (n % 2) + 1][:, :], bwd, w3[:, 1, :], start=True, stop=True).then_inc(pe_k, 1)
                    pe.wait_ge(pl_ok, i * 10 + 10)
                    for j in range(10):
                        pe.wait_ge(w_split, i * 10 + (e0 + j + 1))
                        if j >= 4:
                            pe.wait_ge(spec_ev, 1 + i * 10 + (j - 3))
                        even, od = ps[2 * (j % 4)], ps[2 * (j % 4) + 1]
                        taps = range(4) if j < 8 else range(1)
                        base = (0, 4) if j < 8 else (8, 9)
                        for side, out in enumerate((even, od)):
                            last = products(pe, e0 + j, [
                                (side * len(taps) + k, pqh[:, base[side] + k, j % 2, :],
                                 pql[:, base[side] + k, j % 2, :], out) for k in taps], ((0, 512),))
                        last.then_inc(w_used, 1)
        fst.close()
        e0 += E_FILT

        def modulation(dve, done, layer, sc, sh, ln):
            m0 = layer * 48
            scale, shift = mod[:, m0 + sc * 8:m0 + sc * 8 + 8, :], mod[:, m0 + sh * 8:m0 + sh * 8 + 8, :]
            dve.tensor_scalar(aff[:, 0, :, :], scale, 1.0, None, ALU.add).then_inc(done, 1)
            dve.wait_ge(done, 1)
            if ln is None:
                dve.tensor_copy(aff[:, 1, :, :], shift).then_inc(done, 4)
            else:
                g = ln_p[:, ln, :].unsqueeze(2).to_broadcast([128, 8, 2])
                b = ln_p[:, ln + 1, :].unsqueeze(2).to_broadcast([128, 8, 2])
                dve.tensor_tensor(aff[:, 1, :, :], aff[:, 0, :, :], b, ALU.mult).then_inc(done, 1)
                dve.wait_ge(done, 2)
                dve.tensor_tensor(aff[:, 1, :, :], aff[:, 1, :, :], shift, ALU.add).then_inc(done, 1)
                dve.tensor_tensor(aff[:, 0, :, :], aff[:, 0, :, :], g, ALU.mult).then_inc(done, 1)
                dve.tensor_scalar(axs[:, :, :], ln_p[:, ln:ln + 2, :], ALPHA, None, ALU.mult).then_inc(done, 1)
            dve.wait_ge(done, 5)

        with stage() as st:
            xin = sb("xin", [128, 2, TOK], F32, st)
            xm = sb("xm", [128, 2, TOK], F32, st)
            x_in, coef, xm_ok, xh_ok, xl_ok = [sem("x_in0", st), sem("x_in1", st)], sem("coef", st), sem("xm_ok", st), sem("xh_ok", st), sem("xl_ok", st)
            block = st.enter_context(nc.Block())

            @block.sync
            def _(sp):
                for k in range(KT):
                    if k >= 2:
                        sp.wait_ge(xm_ok, k - 1)
                        sp.wait_ge(xh_ok, k - 1)
                    sp.dma_start(xin[:, k % 2, :], t["x"][k, :, :]).then_inc(x_in[k % 2], 16)

            @block.vector
            def _(dve):
                modulation(dve, coef, 0, SC1, SH1, None)
                for k in range(KT):
                    dve.wait_ge(x_in[k % 2], 16 * (k // 2) + 16)
                    if k >= 2:
                        dve.wait_ge(xl_ok, k - 1)
                    for p, (p0, p1) in enumerate(PARTS):
                        ins = dve.tensor_scalar(xm[:, k % 2, p0:p1], xin[:, k % 2, p0:p1], aff[:, 0, k, p:p + 1],
                                                aff[:, 1, k, p:p + 1], ALU.mult, ALU.add)
                    ins.then_inc(xm_ok, 1)

            @block.scalar
            def _(act):
                act.wait_ge(coef, 5)
                for k in range(KT):
                    act.wait_ge(x_in[k % 2], 16 * (k // 2) + 16)
                    for p, (p0, p1) in enumerate(PARTS):
                        ins = act.activation(a_h[:, k, p0:p1], xin[:, k % 2, p0:p1], ACT.Identity,
                                             scale=aff[:, 0, k, p:p + 1], bias=aff[:, 1, k, p:p + 1])
                    ins.then_inc(xh_ok, 1)

            @block.gpsimd
            def _(pool):
                for k in range(KT):
                    pool.wait_ge(xm_ok, k + 1)
                    pool.wait_ge(xh_ok, k + 1)
                    pool.tensor_tensor(a_l[:, k, :], xm[:, k % 2, :], a_h[:, k, :].bitcast(F32),
                                       ALU.subtract).then_inc(xl_ok, 1)

        tst = ExitStack()
        t_h = sb("t_hi", [128, 10, D], F32R, tst)
        t_l = sb("t_lo", [128, 10, D], F32R, tst)
        with stage() as st:
            za = sb("za", [128, TOK], F32, st)
            zb = sb("zb", [128, TOK], F32, st)
            awr = sb("ada_raw1", [128, 2, 1024], F32, st)
            pg = [st.enter_context(nc.psum_tensor(f"ps_in{g}", [128, 1536], F32)) for g in range(2)]
            pt = st.enter_context(nc.psum_tensor("ps_tr", [128, 512], F32))
            pa = st.enter_context(nc.psum_tensor("ps_ad", [128, 512], F32))
            z_ok, conv, cst, s_ok, fold, tr, th_ok, tl_ok, s_out, x0_out, a_in, pe_a, ad_ok = [
                sem(n, st) for n in ("z_ok", "conv", "cst", "s_ok", "fold", "tr", "th_ok", "tl_ok", "s_out", "x0_out",
                                 "a_in", "pe_a", "ad_ok")]
            a_in = [a_in, sem("a_in1", st)]
            block = st.enter_context(nc.Block())
            TR = ((0, 4, pt), (4, 8, pt), (8, 10, pa))

            @block.sync
            def _(sp):
                sp.sem_inc(x0_out, 1)
                with sp.Fori(0, 4) as i:
                    for cc in range(2):
                        for role in range(3):
                            j = 3 * cc + role
                            load_entry(sp, e0 + 2 + j, wsrc(i * 6 + (e0 + 2 + j)), i, 6)
                            if role == 1:
                                sp.wait_ge(s_ok, i * 2 + (cc + 1))
                                sp.dma_start(s_d[i * 2 + cc, :, :], zb[:, :]).then_inc(s_out, 16)
                            if role == 2:
                                sp.wait_ge(conv, 1 + i * 6 + (3 * cc + 3))
                                sp.dma_start(x0_d[i * 2 + cc, :, :], zb[:, :]).then_inc(x0_out, 16)
                sp.wait_ge(s_out, 128)
                sp.wait_ge(x0_out, 1 + 128)

            @block.gpsimd
            def _(pool):
                with pool.Fori(0, 4) as i:
                    for j in range(6):
                        split_lo(pool, e0 + 2 + j, i, 6)

            @block.scalar
            def _(act):
                with act.Fori(0, 4) as i:
                    for cc in range(2):
                        act.wait_ge(pe_a, 1 + i * 20 + 10 * cc)
                        for n in range(2):
                            act.dma_start(awr[:, n, :], t["ada"][i * 20 + (16 + 10 * cc + n), :, :]).then_inc(
                                a_in[n], 16)
                        for role in range(3):
                            j = 3 * cc + role
                            split_hi(act, e0 + 2 + j, i, 6)
                            act.wait_ge(w_used, i * 6 + (e0 + j + 1))
                            if role == 0:
                                act.wait_ge(tr, 1 + i * 6 + 3 * cc)
                                dst = za
                            elif role == 1:
                                act.wait_ge(x0_out, 1 + i * 32 + 16 * cc)
                                dst = zb
                            else:
                                act.wait_ge(s_out, i * 32 + (16 * cc + 16))
                                act.wait_ge(fold, i * 2 + (cc + 1))
                                dst = zb
                            tile = conv_p[:, bass.ds(i * 6 + j, 1), :]
                            act.activation(dst[:, :], pg[j % 2][:, 0:TOK], ACT.Identity,
                                           scale=tile[:, 0, 1:2], bias=tile[:, 0, 3:4]).then_inc(z_ok, 1)
                        for r, (b0, b1, bank) in enumerate(TR):
                            if r == 1:
                                for n in range(2, 10):
                                    m = 10 * cc + n
                                    act.wait_ge(pe_a, 1 + i * 20 + (m - 1))
                                    act.dma_start(awr[:, n % 2, :], t["ada"][i * 20 + (16 + m), :, :]).then_inc(
                                        a_in[n % 2], 16)
                            act.wait_ge(tr, 1 + i * 6 + (3 * cc + r + 1))
                            act.activation(t_h[:, b0:b1, bass.ds(i * 256 + 128 * cc, 128)],
                                           bank[:, 0:128 * (b1 - b0)].rearrange("p (b c) -> p b c", c=128),
                                           ACT.Copy).then_inc(th_ok, 1)

            @block.vector
            def _(dve):
                dve.sem_inc(conv, 1)
                dve.sem_inc(tl_ok, 1)
                with dve.Fori(0, 4) as i:
                    for cc in range(2):
                        for role in range(3):
                            j = 3 * cc + role
                            z, src = (za, zb, zb)[role], pg[j % 2]
                            w = conv_p[:, bass.ds(i * 6 + j, 1), :]
                            dve.wait_ge(z_ok, i * 6 + (j + 1))
                            for n, (p0, p1) in enumerate(PARTS):
                                ins = dve.scalar_tensor_tensor(z[:, p0 + 1:p1], src[:, p0:p1 - 1], w[:, 0, 0:1],
                                                               z[:, p0 + 1:p1], ALU.mult, ALU.add)
                            ins.then_inc(cst, 1)
                            dve.wait_ge(cst, i * 6 + (j + 1))
                            for n, (p0, p1) in enumerate(PARTS):
                                ins = dve.scalar_tensor_tensor(z[:, p0:p1 - 1], src[:, p0 + 1:p1], w[:, 0, 2:3],
                                                               z[:, p0:p1 - 1], ALU.mult, ALU.add)
                            ins.then_inc(conv, 1)
                            if role == 1:
                                dve.wait_ge(conv, 1 + i * 6 + (j + 1))
                                dve.tensor_tensor(zb[:, :], zb[:, :], za[:, :], ALU.mult).then_inc(s_ok, 1)
                                dve.wait_ge(s_ok, i * 2 + (cc + 1))
                                for p0, p1 in PARTS:
                                    h = (p1 - p0) // 2
                                    back = zb[:, p1 - 1:p0 + h - 1:-1]
                                    dve.tensor_tensor(za[:, p0:p0 + h], zb[:, p0:p0 + h], back, ALU.add)
                                    ins = dve.tensor_tensor(za[:, p0 + h:p1], zb[:, p0:p0 + h], back, ALU.subtract)
                                ins.then_inc(fold, 1)
                        for r, (b0, b1, bank) in enumerate(TR):
                            if r == 1:
                                dve.wait_ge(pe_a, 1 + i * 20 + (10 * cc + 10))
                                dve.tensor_tensor(
                                    mod[:, bass.ds(i * 20 + (16 + 10 * cc), 10), :],
                                    pa[:, 0:20].rearrange("p (a b) -> p a b", b=2),
                                    adab[:, bass.ds(i * 20 + (16 + 10 * cc), 10)].unsqueeze(2).to_broadcast([128, 10, 2]),
                                    ALU.add).then_inc(ad_ok, 1)
                            dve.wait_ge(th_ok, i * 6 + (3 * cc + r + 1))
                            cs = bass.ds(i * 256 + 128 * cc, 128)
                            dve.tensor_tensor(t_l[:, b0:b1, cs],
                                              bank[:, 0:128 * (b1 - b0)].rearrange("p (b c) -> p b c", c=128),
                                              t_h[:, b0:b1, cs].bitcast(F32), ALU.subtract).then_inc(tl_ok, 1)

            @block.tensor
            def _(pe):
                pe.sem_inc(tr, 1)
                pe.sem_inc(pe_a, 1)
                with pe.Fori(0, 4) as i:
                    for cc in range(2):
                        for role in range(3):
                            j = 3 * cc + role
                            pe.wait_ge(w_split, i * 6 + (e0 + j + 1))
                            if j >= 2:
                                pe.wait_ge(conv, 1 + i * 6 + (j - 1))
                            elif role < 2:
                                pe.wait_ge(conv, 1 + i * 6)
                            products(pe, e0 + j, [(k, a_h[:, k, :], a_l[:, k, :], pg[j % 2]) for k in range(KT)],
                                     CHUNKS).then_inc(w_used, 1)
                        pe.wait_ge(fold, i * 2 + (cc + 1))
                        for r, (b0, b1, bank) in enumerate(TR):
                            if r == 1:
                                pe.wait_ge(tl_ok, 1 + i * 6 + 3 * cc)
                                for n in range(10):
                                    m = 10 * cc + n
                                    pe.wait_ge(a_in[n % 2], i * 160 + (16 * (m // 2) + 16))
                                    for k in range(8):
                                        last = pe.matmul(pa[:, 2 * n:2 * n + 2], awr[:, n % 2, k * 128:k * 128 + 128],
                                                         silc[:, k, :], start=k == 0, stop=k == 7)
                                    last.then_inc(pe_a, 1)
                            if r == 2:
                                pe.wait_ge(ad_ok, i * 2 + (cc + 1))
                            else:
                                pe.wait_ge(tl_ok, 1 + i * 6 + (3 * cc + r))
                            for b in range(b0, b1):
                                last = pe.transpose(bank[:, (b - b0) * 128:(b - b0) * 128 + 128],
                                                    za[:, b * 128:b * 128 + 128], ident[:, :])
                            last.then_inc(tr, 1)
        e0 += E_IN
        if t.get("stop_after") == "in":
            tst.close()
            return

        with stage() as st:
            gsl = sb("g_spec", [128, 2, 2, 512], F32, st)
            yb = sb("y_spec", [128, 2, 2, 512], F32, st)
            pr = sb("y_prod", [128, 2, 512], F32, st)
            pf = [st.enter_context(nc.psum_tensor(f"ps_fw{g}", [128, 2048], F32)) for g in range(2)]
            g_in, y_out = [sem("g_in0", st), sem("g_in1", st)], [sem("y_out0", st), sem("y_out1", st)]
            pr_ok, y_ok = sem("pr_ok", st), sem("y_ok", st)
            block = st.enter_context(nc.Block())

            def rounds(step, eng):
                with eng.Fori(0, 3) as i:
                    step(0, i)
                    step(1, i)
                for f in range(6, 10):
                    step(f, None)

            @block.sync
            def _(sp):
                sp.sem_inc(y_out[0], 1)
                sp.sem_inc(y_out[1], 1)

                def step(f, i):
                    if f < 7:
                        load_entry(sp, e0 + 2 + f, wsrc(at(e0 + 2 + f, i, 2)), i, 2)
                    for hf in range(2):
                        sp.wait_ge(y_ok, at(1 + 2 * f + hf + 1, i, 4))
                        for pm in range(2):
                            if f < 8:
                                dst = y_d[4 * hf:4 * hf + 4, (pm + f) % 2, :, at(f, i, 2), :]
                            else:
                                dst = y_d[4 * hf:4 * hf + 4, 2, :, 2 * (f - 8) + pm, :]
                            sp.dma_start(dst.rearrange("c p n -> p c n"),
                                         yb[:, hf, pm, :].rearrange("p (c n) -> p c n", n=128)).then_inc(y_out[hf], 16)
                rounds(step, sp)
                for hf in range(2):
                    sp.wait_ge(y_out[hf], 321)

            @block.scalar
            def _(act):
                def step(f, i):
                    for hf in range(2):
                        act.wait_ge(pr_ok, at(2 * f + hf + 2, i, 4))
                        act.dma_start(gsl[:, hf, :, :], spec[at(f, i, 2), :, :, hf * 512:hf * 512 + 512]).then_inc(
                            g_in[hf], 16)
                    if f < 7:
                        split_hi(act, e0 + 2 + f, i, 2)
                rounds(step, act)

            @block.gpsimd
            def _(pool):
                pool.sem_inc(y_ok, 1)

                def step(f, i):
                    for hf in range(2):
                        pool.wait_ge(pr_ok, at(2 * f + hf + 4, i, 4))
                        pool.tensor_tensor(yb[:, hf, 0, :], yb[:, hf, 0, :], pr[:, 0, :], ALU.add)
                        pool.tensor_tensor(yb[:, hf, 1, :], yb[:, hf, 1, :], pr[:, 1, :],
                                           ALU.subtract).then_inc(y_ok, 1)
                    if f < 7:
                        split_lo(pool, e0 + 2 + f, i, 2)
                rounds(step, pool)

            @block.vector
            def _(dve):
                dve.sem_inc(pr_ok, 3)

                def step(f, i):
                    dve.wait_ge(w_used, at(e0 + min(f, 8) + 1, i, 2))
                    for hf in range(2):
                        c0, c1 = hf * 512, hf * 512 + 512
                        p, m = pf[f % 2][:, c0:c1], pf[f % 2][:, 1024 + c0:1024 + c1]
                        dve.wait_ge(g_in[hf], at(16 * f + 16, i, 32))
                        dve.wait_ge(y_out[hf], at(1 + 32 * f, i, 64))
                        dve.wait_ge(y_ok, at(1 + 2 * f + hf, i, 4))
                        dve.tensor_tensor(yb[:, hf, 0, :], p, gsl[:, hf, 0, :], ALU.mult)
                        dve.tensor_tensor(pr[:, 0, :], m, gsl[:, hf, 1, :], ALU.mult)
                        dve.tensor_tensor(yb[:, hf, 1, :], m, gsl[:, hf, 0, :], ALU.mult)
                        dve.tensor_tensor(pr[:, 1, :], p, gsl[:, hf, 1, :], ALU.mult).then_inc(pr_ok, 1)
                rounds(step, dve)

            @block.tensor
            def _(pe):
                def step(f, i):
                    if f == 9:
                        return
                    pe.wait_ge(w_split, at(e0 + f + 1, i, 2))
                    pe.wait_ge(pr_ok, at(2 * f + 1, i, 4) if f < 8 else 2 * f + 3)
                    if f < 8:
                        for pm in range(2):
                            base = 4 * ((pm + f) % 2)
                            last = products(pe, e0 + f, [
                                (4 * pm + k, t_h[:, base + k, :], t_l[:, base + k, :],
                                 pf[f % 2][:, pm * 1024:pm * 1024 + 1024]) for k in range(4)], ((0, 512), (512, 1024)))
                    else:
                        for ab in range(2):
                            for pm in range(2):
                                last = products(pe, e0 + 8, [
                                    (4 * ab + 2 * pm + k, t_h[:, 8 + k, :], t_l[:, 8 + k, :],
                                     pf[ab][:, pm * 1024:pm * 1024 + 1024]) for k in range(2)], ((0, 512), (512, 1024)))
                    last.then_inc(w_used, 1)
                rounds(step, pe)
        tst.close()
        e0 += E_FWD
        if t.get("stop_after") == "fwd":
            return

        w0 = e0
        with stage() as st:
            ib_h = sb("ib_hi", [128, 18, 512], F32R, st)
            ib_l = sb("ib_lo", [128, 18, 512], F32R, st)
            sx = sb("sx", [128, 2, 2 * TOK], F32, st)
            yt = sb("yt", [128, TOK], F32, st)
            an = sb("anti", [128, 512], F32, st)
            pi = [st.enter_context(nc.psum_tensor(f"ps_iv{g}", [128, 1536], F32)) for g in range(2)]
            b_in, bh_ok, bl_ok, sx_in, an_ok, yp_ok, ya, yb2, g_ok, ah_ok, al_ok = [
                sem(n, st) for n in ("b_in", "bh_ok", "bl_ok", "sx_in", "an_ok", "yp_ok", "ya", "yb", "g_ok", "ah_ok", "al_ok")]
            b_in, sx_in = [b_in, sem("b_in1", st)], [sx_in, sem("sx_in1", st)]
            block = st.enter_context(nc.Block())

            def rounds(step, eng):
                with eng.Fori(0, 3) as i:
                    step(0, i)
                    step(1, i)
                step(6, None)
                step(7, None)

            @block.sync
            def _(sp):
                for j in range(2):
                    load_entry(sp, e0 + j, y_d[0, j, :, :, :].rearrange("p f n -> p (f n)"))
                for n in range(5):
                    if n >= 2:
                        sp.wait_ge(bl_ok, n - 1)
                    src = t["inv"][n, :, :] if n < 4 else t["inv_p"]
                    sp.dma_start(sx[:, n % 2, 0:src.shape[1]], src).then_inc(b_in[n % 2], 16)
                sp.wait_ge(bl_ok, 5)

                def step(c, i):
                    sp.wait_ge(al_ok, at(c + 1, i, 2))
                    sp.dma_start(sx[:, c % 2, 0:TOK], s_d[at(c, i, 2), :, :]).then_inc(sx_in[c % 2], 16)
                    sp.dma_start(sx[:, c % 2, TOK:2 * TOK], x0_d[at(c, i, 2), :, :]).then_inc(sx_in[c % 2], 16)
                    for j in range(3):
                        n = 3 * c + j + 2
                        if n < E_INV:
                            src = y_d[at(n // 3, i, 2), n % 3, :, :, :].rearrange("p f n -> p (f n)")
                            width = 512 if n % 3 == 2 else 1024
                            load_entry(sp, e0 + n, src[:, 0:width], i, 6, width)
                        else:
                            load_entry(sp, e0 + n, wsrc(w0 + n - E_INV), i, 6)
                rounds(step, sp)

            @block.gpsimd
            def _(pool):
                split_lo(pool, e0)
                split_lo(pool, e0 + 1)

                def step(c, i):
                    for j in range(3):
                        n = 3 * c + j + 2
                        split_lo(pool, e0 + n, i, 6, 512 if n < E_INV and n % 3 == 2 else 1024)
                rounds(step, pool)

            @block.scalar
            def _(act):
                split_hi(act, e0)
                split_hi(act, e0 + 1)
                for n in range(5):
                    w = 4 if n < 4 else 2
                    act.wait_ge(b_in[n % 2], 16 * (n // 2) + 16)
                    act.activation(ib_h[:, 4 * n:4 * n + w, :],
                                   sx[:, n % 2, 0:512 * w].rearrange("p (a b) -> p a b", b=512),
                                   ACT.Copy).then_inc(bh_ok, 1)

                def step(c, i):
                    for j in range(3):
                        n = 3 * c + j + 2
                        split_hi(act, e0 + n, i, 6, 512 if n < E_INV and n % 3 == 2 else 1024)
                        act.wait_ge(w_used, at(e0 + 3 * c + j + 1, i, 6))
                        if j == 1:
                            act.wait_ge(al_ok, at(c + 2, i, 2))
                            act.activation(an[:, :], pi[c % 2][:, 512:1024], ACT.Copy).then_inc(an_ok, 1)
                        if j == 2:
                            act.activation(yt[:, LS:TOK], pi[c % 2][:, 1024:1280], ACT.Copy).then_inc(yp_ok, 1)
                    act.wait_ge(g_ok, at(c + 1, i, 2))
                    act.activation(a_h[:, bass.ds(at(c, i, 2), 1), :], yt[:, :].unsqueeze(1), ACT.Copy).then_inc(ah_ok, 1)
                rounds(step, act)

            @block.vector
            def _(dve):
                dve.sem_inc(al_ok, 2)
                for n in range(5):
                    w = 4 if n < 4 else 2
                    dve.wait_ge(bh_ok, n + 1)
                    dve.tensor_tensor(ib_l[:, 4 * n:4 * n + w, :],
                                      sx[:, n % 2, 0:512 * w].rearrange("p (a b) -> p a b", b=512),
                                      ib_h[:, 4 * n:4 * n + w, :].bitcast(F32), ALU.subtract).then_inc(bl_ok, 1)

                def step(c, i):
                    sym = pi[c % 2][:, 0:512]
                    dve.wait_ge(an_ok, at(c + 1, i, 2))
                    dve.tensor_tensor(yt[:, 0:512], sym, an[:, :], ALU.add)
                    dve.tensor_tensor(yt[:, 1023:511:-1], sym, an[:, :], ALU.subtract).then_inc(ya, 1)
                    dve.wait_ge(ya, at(c + 1, i, 2))
                    dve.wait_ge(yp_ok, at(c + 1, i, 2))
                    dve.wait_ge(sx_in[c % 2], at(32 * (c // 2) + 32, i, 32))
                    dve.scalar_tensor_tensor(yt[:, :], sx[:, c % 2, 0:TOK], hb_p[:, bass.ds(at(c, i, 2), 1)],
                                             yt[:, :], ALU.mult, ALU.add).then_inc(yb2, 1)
                    dve.wait_ge(yb2, at(c + 1, i, 2))
                    dve.tensor_tensor(yt[:, :], yt[:, :], sx[:, c % 2, TOK:2 * TOK], ALU.mult).then_inc(g_ok, 1)
                    dve.wait_ge(g_ok, at(c + 1, i, 2))
                    dve.wait_ge(ah_ok, at(c + 1, i, 2))
                    dve.tensor_tensor(a_l[:, bass.ds(at(c, i, 2), 1), :], yt[:, :].unsqueeze(1),
                                      a_h[:, bass.ds(at(c, i, 2), 1), :].bitcast(F32), ALU.subtract).then_inc(al_ok, 1)
                rounds(step, dve)

            @block.tensor
            def _(pe):
                pe.wait_ge(bl_ok, 5)

                def step(c, i):
                    out = pi[c % 2]
                    for j in range(3):
                        pe.wait_ge(w_split, at(e0 + 3 * c + j + 1, i, 6))
                        if j == 0:
                            pe.wait_ge(al_ok, at(c + 1, i, 2))
                        if j < 2:
                            use = [2 * f + (f + j) % 2 for f in range(8)]
                            last = products(pe, e0 + 3 * c + j, [
                                (f, ib_h[:, u, :], ib_l[:, u, :], out[:, 512 * j:512 * j + 512])
                                for f, u in enumerate(use)], ((0, 512),))
                        else:
                            bh = ib_h[:, 16:18, :].rearrange("p a (b n) -> p (a b) n", n=256)
                            bl = ib_l[:, 16:18, :].rearrange("p a (b n) -> p (a b) n", n=256)
                            last = products(pe, e0 + 3 * c + 2, [
                                (b, bh[:, b, :], bl[:, b, :], out[:, 1024:1280]) for b in range(4)], ((0, 256),))
                        last.then_inc(w_used, 1)
                rounds(step, pe)
        e0 += E_INV
        wsh = E_INV

        def stage_out(layer, e0, xt, s1, s2):
            with stage() as st:
                sq = sb("sq", [128, 2, TOK], F32, st)
                pg = [st.enter_context(nc.psum_tensor(f"ps_out{layer}{g}", [128, 1536], F32)) for g in range(2)]
                x_in, xs_ok, x_ok, sq_ok, s1_ok, s2_ok = [
                    sem(n, st) for n in ("x_in", "xs_ok", "x_ok", "sq_ok", "s1_ok", "s2_ok")]
                block = st.enter_context(nc.Block())

                @block.sync
                def _(sp):
                    src = t["x"] if layer == 0 else x_d
                    for k in range(KT):
                        sp.dma_start(xt[:, k, :], src[k, :, :]).then_inc(x_in, 16)
                    with sp.Fori(0, 4) as i:
                        for j in range(2):
                            load_entry(sp, e0 + 2 + j, wsrc(i * 2 + (e0 + 2 + j - wsh)), i, 2)

                @block.gpsimd
                def _(pool):
                    pool.memset(s1[:, :], 0.0).then_inc(s1_ok, 1)
                    with pool.Fori(0, 4) as i:
                        for j in range(2):
                            pool.wait_ge(x_ok, i * 2 + (j + 3))
                            pool.wait_ge(s1_ok, i * 2 + (j + 1))
                            pool.tensor_tensor(s1[:, :], s1[:, :], xt[:, i * 2 + j, :], ALU.add).then_inc(s1_ok, 1)
                            split_lo(pool, e0 + 2 + j, i, 2)

                @block.scalar
                def _(act):
                    act.wait_ge(x_in, 128)
                    if layer == 0:
                        act.activation(xt[:, :, :], xt[:, :, :], ACT.Copy, scale=ALPHA).then_inc(xs_ok, 1)
                    else:
                        act.sem_inc(xs_ok, 1)
                    with act.Fori(0, 4) as i:
                        for j in range(2):
                            split_hi(act, e0 + 2 + j, i, 2)
                            act.wait_ge(x_ok, i * 2 + (j + 3))
                            act.wait_ge(s2_ok, i * 2 + (j + 1))
                            act.activation(sq[:, j, :], xt[:, i * 2 + j, :], ACT.Square).then_inc(sq_ok, 1)

                @block.vector
                def _(dve):
                    dve.sem_inc(x_ok, 2)
                    dve.memset(s2[:, :], 0.0).then_inc(s2_ok, 2)
                    dve.wait_ge(xs_ok, 1)
                    with dve.Fori(0, 4) as i:
                        for j in range(2):
                            dve.wait_ge(w_used, i * 2 + (e0 + j + 1))
                            gate = mod[:, bass.ds(i * 2 + (layer * 48 + G1 * 8 + j), 1), :]
                            for p, (p0, p1) in enumerate(PARTS):
                                ins = dve.scalar_tensor_tensor(xt[:, i * 2 + j, p0:p1], pg[j][:, p0:p1],
                                                               gate[:, 0, p:p + 1], xt[:, i * 2 + j, p0:p1],
                                                               ALU.mult, ALU.add)
                            ins.then_inc(x_ok, 1)
                            dve.wait_ge(sq_ok, i * 2 + (j + 1))
                            dve.wait_ge(s2_ok, i * 2 + (j + 2))
                            dve.tensor_tensor(s2[:, :], s2[:, :], sq[:, j, :], ALU.add).then_inc(s2_ok, 1)

                @block.tensor
                def _(pe):
                    with pe.Fori(0, 4) as i:
                        for j in range(2):
                            pe.wait_ge(w_split, i * 2 + (e0 + j + 1))
                            pe.wait_ge(x_ok, i * 2 + (j + 1))
                            products(pe, e0 + j, [(k, a_h[:, k, :], a_l[:, k, :], pg[j]) for k in range(KT)],
                                     CHUNKS).then_inc(w_used, 1)

        def stage_norm(layer, ln, xt, s1, s2, then):
            with stage() as st:
                mu = sb("mu", [128, TOK], F32, st)
                rstd = sb("rstd", [128, TOK], F32, st)
                xn = sb("xn", [128, 2, TOK], F32, st)
                xm = sb("xm2", [128, 2, TOK], F32, st)
                pm = st.enter_context(nc.psum_tensor(f"ps_mean{layer}{ln}", [128, 1536], F32))
                pv = st.enter_context(nc.psum_tensor(f"ps_sq{layer}{ln}", [128, 1536], F32))
                stat, mu_ok, v_ok, sd_ok, rs_ok, coef, xc_ok, xn_ok, xm_ok, xh_ok, xl_ok, xa_ok, x_out = [
                    sem(n, st) for n in ("stat", "mu_ok", "v_ok", "sd_ok", "rs_ok", "coef", "xc_ok", "xn_ok", "xm_ok", "xh_ok",
                                     "xl_ok", "xa_ok", "x_out")]
                block = st.enter_context(nc.Block())

                @block.sync
                def _(sp):
                    if then != "ffn":
                        dst = x_d if then == "qkv" else t["y"]
                        for k in range(KT):
                            sp.wait_ge(xa_ok, k + 1)
                            sp.dma_start(dst[k, :, :], xt[:, k, :]).then_inc(x_out, 16)
                        sp.wait_ge(x_out, 128)

                @block.tensor
                def _(pe):
                    for ps, src in ((pm, s1), (pv, s2)):
                        for c0, c1 in CHUNKS:
                            last = pe.matmul(ps[:, c0:c1], meanw[:, :], src[:, c0:c1], start=True, stop=True)
                        last.then_inc(stat, 1)

                @block.scalar
                def _(act):
                    act.wait_ge(stat, 1)
                    act.activation(mu[:, :], pm[:, 0:TOK], ACT.Copy).then_inc(mu_ok, 1)
                    act.wait_ge(v_ok, 3)
                    act.activation(rstd[:, :], rstd[:, :], ACT.Sqrt, bias=eps[:, :]).then_inc(sd_ok, 1)
                    for k in range(KT):
                        act.wait_ge(xn_ok, k + 1)
                        if then != "end":
                            for p, (p0, p1) in enumerate(PARTS):
                                ins = act.activation(a_h[:, k, p0:p1], xn[:, k % 2, p0:p1], ACT.Identity,
                                                     scale=aff[:, 0, k, p:p + 1], bias=aff[:, 1, k, p:p + 1])
                            ins.then_inc(xh_ok, 1)
                            g, b = axs[:, 0, k:k + 1], axs[:, 1, k:k + 1]
                        else:
                            g, b = ln_p[:, ln, k:k + 1], ln_p[:, ln + 1, k:k + 1]
                        act.activation(xt[:, k, :], xn[:, k % 2, :], ACT.Identity, scale=g, bias=b).then_inc(xa_ok, 1)

                @block.vector
                def _(dve):
                    if then == "ffn":
                        modulation(dve, coef, layer, SC2, SH2, ln)
                    elif then == "qkv":
                        modulation(dve, coef, 1, SC1, SH1, ln)
                    dve.wait_ge(mu_ok, 1)
                    dve.tensor_tensor(rstd[:, :], mu[:, :], mu[:, :], ALU.mult).then_inc(v_ok, 1)
                    dve.wait_ge(v_ok, 1)
                    dve.wait_ge(stat, 2)
                    dve.tensor_tensor(rstd[:, :], pv[:, 0:TOK], rstd[:, :], ALU.subtract).then_inc(v_ok, 1)
                    dve.wait_ge(v_ok, 2)
                    dve.tensor_scalar(rstd[:, :], rstd[:, :], 0.0, None, ALU.max).then_inc(v_ok, 1)
                    dve.wait_ge(sd_ok, 1)
                    dve.reciprocal(rstd[:, :], rstd[:, :]).then_inc(rs_ok, 1)
                    dve.wait_ge(rs_ok, 1)
                    for k in range(KT + 1):
                        if k < KT:
                            if k >= 2:
                                dve.wait_ge(xa_ok, k - 1)
                            dve.tensor_tensor(xn[:, k % 2, :], xt[:, k, :], mu[:, :], ALU.subtract).then_inc(xc_ok, 1)
                            dve.wait_ge(xc_ok, k + 1)
                            dve.tensor_tensor(xn[:, k % 2, :], xn[:, k % 2, :], rstd[:, :], ALU.mult).then_inc(xn_ok, 1)
                        if k >= 1 and then != "end":
                            if k >= 3:
                                dve.wait_ge(xl_ok, k - 2)
                            dve.wait_ge(xn_ok, k)
                            for p, (p0, p1) in enumerate(PARTS):
                                ins = dve.tensor_scalar(xm[:, (k - 1) % 2, p0:p1], xn[:, (k - 1) % 2, p0:p1],
                                                        aff[:, 0, k - 1, p:p + 1], aff[:, 1, k - 1, p:p + 1],
                                                        ALU.mult, ALU.add)
                            ins.then_inc(xm_ok, 1)
                            dve.wait_ge(xm_ok, k)

                @block.gpsimd
                def _(pool):
                    if then != "end":
                        for k in range(KT):
                            pool.wait_ge(xm_ok, k + 1)
                            pool.wait_ge(xh_ok, k + 1)
                            pool.tensor_tensor(a_l[:, k, :], xm[:, k % 2, :], a_h[:, k, :].bitcast(F32),
                                               ALU.subtract).then_inc(xl_ok, 1)

        def stage_ffn(layer, e0, xt, s1, s2, last_stage):
            with stage() as st:
                hh = sb("hid_hi", [128, 2, 2, TOK], F32R, st)
                hl = sb("hid_lo", [128, 2, 2, TOK], F32R, st)
                sg = sb("silu_g", [128, TOK], F32, st)
                hf = sb("hid", [128, TOK], F32, st)
                pg = [st.enter_context(nc.psum_tensor(f"ps_ff{layer}{g}", [128, 1536], F32)) for g in range(2)]
                silu, gated, hh_ok, hl_ok, out_mm, out_ok, sq_ok, s1_ok, s2_ok = [
                    sem(n, st) for n in ("silu", "gated", "hh_ok", "hl_ok", "out_mm", "out_ok", "sq_ok", "s1_ok", "s2_ok")]
                block = st.enter_context(nc.Block())

                def rounds(step_in, step_out, eng):
                    step_in(0, e0, None)
                    with eng.Fori(0, 5) as r:
                        for q in range(2):
                            step_in(1 + q, e0 + 4 + 6 * q, r)
                            step_out(q, e0 + 8 + 6 * q, r)
                    step_out(FC - 1, e0 + E_FFN - 2, None)

                @block.sync
                def _(sp):
                    def load(n, e, r):
                        for j in range(n):
                            if last_stage and r is None and e + 2 + j >= e0 + E_FFN:
                                continue
                            load_entry(sp, e + 2 + j, wsrc(at(e + 2 + j - wsh, r, 12)), r, 12)
                    rounds(lambda i, e, r: load(4, e, r), lambda i, e, r: load(2, e, r), sp)

                @block.scalar
                def _(act):
                    def step_in(i, e, r):
                        for k in range(2):
                            act.wait_ge(w_used, at(e + 2 * k + 1, r, 12))
                            if not (r is None and k == 0):
                                act.wait_ge(gated, at(2 * i + k, r, 4))
                            act.activation(sg[:, :], pg[0][:, 0:TOK], ACT.Silu).then_inc(silu, 1)
                            split_hi(act, e + 2 + 2 * k, r, 12)
                            act.wait_ge(gated, at(2 * i + k + 1, r, 4))
                            act.activation(hh[:, i % 2, k, :], hf[:, :], ACT.Copy).then_inc(hh_ok, 1)
                            split_hi(act, e + 3 + 2 * k, r, 12)

                    def step_out(i, e, r):
                        if r is not None:
                            for j in range(2):
                                split_hi(act, e + 2 + j, r, 12)
                        else:
                            for m in range(8):
                                act.wait_ge(out_ok, 8 + 8 * i + m + 1)
                                if m >= 2:
                                    act.wait_ge(s2_ok, m)
                                act.activation((sg, hf)[m % 2][:, :], xt[:, m, :], ACT.Square).then_inc(sq_ok, 1)
                                if m % 4 == 3 and not last_stage:
                                    split_hi(act, e + 2 + m // 4)
                    rounds(step_in, step_out, act)

                @block.gpsimd
                def _(pool):
                    pool.memset(s1[:, :], 0.0).then_inc(s1_ok, 1)

                    def step_in(i, e, r):
                        for k in range(2):
                            split_lo(pool, e + 2 + 2 * k, r, 12)
                            pool.wait_ge(hh_ok, at(2 * i + k + 1, r, 4))
                            pool.tensor_tensor(hl[:, i % 2, k, :], hf[:, :], hh[:, i % 2, k, :].bitcast(F32),
                                               ALU.subtract).then_inc(hl_ok, 1)
                            split_lo(pool, e + 3 + 2 * k, r, 12)

                    def step_out(i, e, r):
                        if r is not None:
                            for j in range(2):
                                split_lo(pool, e + 2 + j, r, 12)
                        else:
                            for m in range(8):
                                pool.wait_ge(out_ok, 8 + 8 * i + m + 1)
                                pool.wait_ge(s1_ok, m + 1)
                                pool.tensor_tensor(s1[:, :], s1[:, :], xt[:, m, :], ALU.add).then_inc(s1_ok, 1)
                                if m % 4 == 3 and not last_stage:
                                    split_lo(pool, e + 2 + m // 4)
                    rounds(step_in, step_out, pool)

                @block.vector
                def _(dve):
                    dve.sem_inc(out_ok, 8)
                    dve.memset(s2[:, :], 0.0).then_inc(s2_ok, 1)

                    def step_in(i, e, r):
                        for k in range(2):
                            dve.wait_ge(w_used, at(e + 2 * k + 2, r, 12))
                            dve.wait_ge(silu, at(2 * i + k + 1, r, 4))
                            if not (r is None and k == 0):
                                dve.wait_ge(hl_ok, at(2 * i + k, r, 4))
                            dve.tensor_tensor(hf[:, :], sg[:, :], pg[1][:, 0:TOK], ALU.mult).then_inc(gated, 1)

                    def step_out(i, e, r):
                        for m in range(8):
                            if m % 4 == 3:
                                dve.wait_ge(w_used, at(e + m // 4 + 1, r, 12))
                            else:
                                dve.wait_ge(out_mm, at(6 * i + 3 * (m // 4) + m % 4 + 1, r, 12))
                            gate = mod[:, layer * 48 + G2 * 8 + m, :]
                            if i or r is not None:
                                dve.wait_ge(out_ok, at(8 + 8 * i + m - 7, r, 16))
                            for p, (p0, p1) in enumerate(PARTS):
                                ins = dve.scalar_tensor_tensor(xt[:, m, p0:p1], pg[m % 2][:, p0:p1], gate[:, p:p + 1],
                                                               xt[:, m, p0:p1], ALU.mult, ALU.add)
                            ins.then_inc(out_ok, 1)
                            if r is None and m >= 1:
                                dve.wait_ge(sq_ok, m)
                                dve.wait_ge(s2_ok, m)
                                dve.tensor_tensor(s2[:, :], s2[:, :], (sg, hf)[(m - 1) % 2][:, :],
                                                  ALU.add).then_inc(s2_ok, 1)
                        if r is None:
                            dve.wait_ge(sq_ok, 8)
                            dve.wait_ge(s2_ok, 8)
                            dve.tensor_tensor(s2[:, :], s2[:, :], hf[:, :], ALU.add).then_inc(s2_ok, 1)
                    rounds(step_in, step_out, dve)
                @block.tensor
                def _(pe):
                    def step_in(i, e, r):
                        for j in range(4):
                            pe.wait_ge(w_split, at(e + j + 1, r, 12))
                            if j < 2 and r is not None:
                                pe.wait_ge((silu, gated)[j], at(2 * i, r, 4))
                                pe.wait_ge(out_ok, at(8 * (i - 1) + 7 + j, r, 16))
                            elif j >= 2:
                                pe.wait_ge((silu, gated)[j % 2], at(2 * i + 1, r, 4))
                            products(pe, e + j, [(k, a_h[:, k, :], a_l[:, k, :], pg[j % 2]) for k in range(KT)],
                                     CHUNKS).then_inc(w_used, 1)

                    def step_out(i, e, r):
                        pe.wait_ge(hl_ok, at(2 * i + 2, r, 4))
                        for m in range(8):
                            if m % 4 == 0:
                                pe.wait_ge(w_split, at(e + m // 4 + 1, r, 12))
                            if m < 2 and r is not None:
                                pe.wait_ge((silu, gated)[m], at(2 * i + 4, r, 4))
                            elif m < 2:
                                pe.wait_ge(out_ok, 8 * i + 7 + m)
                            else:
                                pe.wait_ge(out_ok, at(8 + 8 * i + m - 1, r, 16))
                            last = products(pe, e + m // 4, [(2 * (m % 4) + k, hh[:, i % 2, k, :], hl[:, i % 2, k, :],
                                                              pg[m % 2]) for k in range(2)], CHUNKS)
                            last.then_inc(w_used if m % 4 == 3 else out_mm, 1)
                    rounds(step_in, step_out, pe)

        def stage_qkv(e0):
            with stage() as st:
                z = sb("z_qkv", [128, 2, TOK], F32, st)
                pg = [st.enter_context(nc.psum_tensor(f"ps_qkv{g}", [128, 1536], F32)) for g in range(2)]
                z_ok, z_out = [sem("z_ok0", st), sem("z_ok1", st)], [sem("z_out0", st), sem("z_out1", st)]
                block = st.enter_context(nc.Block())

                @block.sync
                def _(sp):
                    for j in range(2):
                        sp.sem_inc(z_out[j], 1)
                    with sp.Fori(0, 12) as i:
                        for j in range(2):
                            load_entry(sp, e0 + 2 + j, wsrc(i * 2 + (e0 + 2 + j - wsh)), i, 2)
                            sp.wait_ge(z_ok[j], i + 2)
                            sp.dma_start(qkv_d[i * 2 + j, :, :], z[:, j, :]).then_inc(z_out[j], 16)
                    for j in range(2):
                        sp.wait_ge(z_out[j], 1 + 16 * 12)

                @block.gpsimd
                def _(pool):
                    with pool.Fori(0, 12) as i:
                        for j in range(2):
                            split_lo(pool, e0 + 2 + j, i, 2)

                @block.scalar
                def _(act):
                    act.sem_inc(z_ok[0], 1)
                    with act.Fori(0, 12) as i:
                        for j in range(2):
                            split_hi(act, e0 + 2 + j, i, 2)
                            if j == 0:
                                act.wait_ge(w_used, i * 2 + (e0 + 1))
                                act.wait_ge(z_out[0], i * 16 + 1)
                                act.activation(z[:, 0, :], pg[0][:, 0:TOK], ACT.Copy).then_inc(z_ok[0], 1)

                @block.vector
                def _(dve):
                    dve.sem_inc(z_ok[1], 1)
                    with dve.Fori(0, 12) as i:
                        dve.wait_ge(w_used, i * 2 + (e0 + 2))
                        dve.wait_ge(z_out[1], i * 16 + 1)
                        dve.tensor_copy(z[:, 1, :], pg[1][:, 0:TOK]).then_inc(z_ok[1], 1)

                @block.tensor
                def _(pe):
                    with pe.Fori(0, 12) as i:
                        for j in range(2):
                            pe.wait_ge(w_split, i * 2 + (e0 + j + 1))
                            pe.wait_ge(z_ok[j], i + 1)
                            products(pe, e0 + j, [(k, a_h[:, k, :], a_l[:, k, :], pg[j]) for k in range(KT)],
                                     CHUNKS).then_inc(w_used, 1)

        def layer_rest(layer, e0):
            with ExitStack() as st:
                xt = sb("x_t", [128, KT, TOK], F32, st)
                s1 = sb("sum_x", [128, TOK], F32, st)
                s2 = sb("sum_xx", [128, TOK], F32, st)
                stage_out(layer, e0, xt, s1, s2)
                stage_norm(layer, 4 * layer, xt, s1, s2, "ffn")
                stage_ffn(layer, e0 + E_OUT, xt, s1, s2, layer == 1)
                stage_norm(layer, 4 * layer + 2, xt, s1, s2, "end" if layer else "qkv")
            return e0 + E_OUT + E_FFN

        e0 = layer_rest(0, e0)
        stage_qkv(e0)
        e0 += E_QKV
        if t.get("stop_after") == "qkv":
            return

        with stage() as st:
            U = 20
            qr = sb("q_raw", [128, TOK], F32, st)
            kr = sb("k_raw", [128, 2560], F32, st)
            qh = sb("q_hl", [128, 2, TOK], F32R, st)
            kh = sb("k_hi", [128, 2, 1536], F32R, st)
            kl = sb("k_lo", [128, 2, 1536], F32R, st)
            vh = sb("v_hi", [128, 20, 128], F32R, st)
            vl = sb("v_lo", [128, 20, 128], F32R, st)
            bias = sb("rpb_t", [128, 2, 16, RPB_W], F32, st)
            pb = sb("probs", [128, 3, 640], F32, st)
            pth = sb("pt_hi", [128, 2, 5, 128], F32R, st)
            ptl = sb("pt_lo", [128, 2, 5, 128], F32R, st)
            mask = sb("mask", [128, 6, 384], BF16, st)
            ident_b = sb("ident_b", [128, 128], BF16, st)
            stat = sb("stat", [128, 3, 8], F32, st)
            ps_s = [st.enter_context(nc.psum_tensor(f"ps_s{b}", [128, 1024], F32)) for b in range(2)]
            ps_t = st.enter_context(nc.psum_tensor("ps_t", [128, 1024], F32))
            ps_o = [st.enter_context(nc.psum_tensor(f"ps_o{b}", [128, 512], F32)) for b in range(2)]
            m_in, mk_ok, kr_in, qr_in, kv_out = [sem(n, st) for n in ("m_in", "mk_ok", "kr_in", "qr_in", "kv_out")]
            b_in = [sem("bias_in0", st), sem("bias_in1", st)]
            vt_mm, vh_ok, vr_ok, qh_ok, qs_ok, kh_ok, kl_ok = [
                sem(n, st) for n in ("vt_mm", "vh_ok", "vr_ok", "qh_ok", "qs_ok", "kh_ok", "kl_ok")]
            s_mm, mx_ok, nm_ok, p_exp, tot_ok, rr_ok, turn, turn_v, pn_ok, t_mm, pth_ok, ptl_ok, pv_mm, oh_ok, ol_ok = [
                sem(n, st) for n in ("s_mm", "mx_ok", "nm_ok", "p_exp", "tot_ok", "rr_ok", "turn", "turn_v", "pn_ok", "t_mm", "pth_ok",
                                 "ptl_ok", "pv_mm", "oh_ok", "ol_ok")]
            QS0, KL0, S0, NM0, EX0, T0, PTL0, PV0, OL0 = 1, 1, 20, 20, 2, 3, 1, 2, 2
            block = st.enter_context(nc.Block())
            V_CTX, V_CACHE = 2048, 2304
            ROUNDS = ((0, 4), (4, 8), (8, 12), (12, 16), (18, 20))

            def unit(u):
                hh, n = u // 10, u % 10
                return (hh, n // 4, n % 4) if n < 8 else (hh, None, n - 8)

            def blocked(ap):
                return ap.rearrange("p (j r c) -> p r j c", j=4, c=16)

            def backwards(ap):
                (ps, pn), (sa, na), (sb_, nb) = ap.ap
                return bass.AP(ap.tensor, ap.offset + (na - 1) * sa + (nb - 1) * sb_, [[ps, pn], [-sa, na], [-sb_, nb]])

            def grid(ap, r0, rows, c0, cols):
                return ap.rearrange("p (r c) -> p r c", c=GW)[:, r0:r0 + rows, c0:c0 + cols]

            @block.sync
            def _(sp):
                flat = t["mask"].rearrange("p a b -> p (a b)")
                for n in range(2):
                    if n:
                        sp.wait_ge(mk_ok, 2)
                    sp.dma_start(pb[:, :, :].rearrange("p a b -> p (a b)")[:, 0:1152],
                                 flat[:, 1152 * n:1152 * n + 1152]).then_inc(m_in, 16)
                for n, name in ((1, "nk"), (2, "nv")):
                    sp.dma_start(t[name], qkv_d[8 * n:8 * n + 8, :, LS:TOK]).then_inc(kv_out, 16)
                with sp.Fori(0, 8) as i:
                    sp.wait_ge(kl_ok, i * 2 + KL0)
                    for b in range(4):
                        sp.dma_start(kr[:, 512 * b:512 * b + 512].rearrange("p (r c) -> p r c", c=32),
                                     grid(qkv_d[i + 16, :, 0:LS], 0, 16, BANDS[b], 32)).then_inc(kr_in, 16)
                    sp.dma_start(kr[:, V_CTX:V_CACHE], qkv_d[i + 16, :, LS:TOK]).then_inc(kr_in, 16)
                    sp.dma_start(kr[:, V_CACHE:2560].rearrange("p (t n) -> p t n", n=128),
                                 t["cache_v"][i, :, :, :]).then_inc(kr_in, 16)
                    for hh in range(2):
                        sp.wait_ge(qs_ok, i * 2 + (QS0 + hh))
                        for half in range(2):
                            sp.dma_start(qr[64 * half:64 * half + 64, :],
                                         qkv_d[i, 64 * hh:64 * hh + 64, :]).then_inc(qr_in, 16)
                        sp.wait_ge(nm_ok, i * 20 + (10 * hh + 8))
                        for r in range(8):
                            table = t["rpb"][i * 2 + hh, :]
                            src = bass.AP(table.tensor, table.offset + ((r + 1) * RPB_W - 15),
                                          [[1, 16], [1, 16 * RPB_W]])
                            sp.dma_start(bias[16 * r:16 * r + 16, hh, :, :].rearrange("p a b -> p (a b)"),
                                         src).then_inc(b_in[hh], 16)
                        if hh == 0:
                            sp.wait_ge(vr_ok, i * 6 + 6)
                        else:
                            sp.wait_ge(kl_ok, i * 2 + (KL0 + 1))
                        for half in range(2):
                            rows = slice(64 * half, 64 * half + 64)
                            k = qkv_d[i + 8, 64 * hh:64 * hh + 64, :]
                            sp.dma_start(kr[rows, 0:LS], k[:, 0:LS]).then_inc(kr_in, 16)
                            sp.dma_start(kr[rows, LS + 256:1536], k[:, LS:TOK]).then_inc(kr_in, 16)
                            sp.dma_start(kr[rows, LS:LS + 256], t["cache_kt"][i * 2 + hh, :, :]).then_inc(kr_in, 16)
                sp.wait_ge(kv_out, 32)

            def out_view(a, i, u):
                hh, half, j = unit(u)
                rows = slice(64 * hh, 64 * hh + 64)
                if half is None:
                    return rows, a[rows, i, LS + 128 * j:LS + 128 * j + 128]
                return rows, grid(a[rows, i, 0:LS], 8 * half, 8, 16 * j, 16)

            def src_view(rows, u):
                src = ps_o[u % 2][rows, 0:128]
                return src if unit(u)[1] is None else src.rearrange("p (r c) -> p r c", c=16)

            def run(eng, per_pair, start, head, steps):
                with eng.Fori(0, 8) as i:
                    if per_pair:
                        per_pair(i)
                    head(i, 0)
                    start(i)
                    for u in range(U + 1):
                        if u == 4:
                            head(i, 1)
                        steps(i, u)

            @block.tensor
            def _(pe):
                pe.sem_inc(s_mm, S0)
                pe.sem_inc(t_mm, T0)
                pe.sem_inc(pv_mm, PV0)

                def per_pair(i):
                    pe.wait_ge(kr_in, i * 288 + 96)
                    for r, (b0, b1) in enumerate(ROUNDS):
                        if r < 2:
                            pe.wait_ge(ptl_ok, i * U + PTL0)
                        else:
                            pe.wait_ge(vr_ok, i * 6 + (r - 1))
                        for b in range(b0, b1):
                            v0 = 128 * b if b < 16 else V_CTX + 128 * (b - 18)
                            src = kr[:, v0:v0 + 128]
                            o = (r % 2) * 512 + (b - b0) * 128
                            last = pe.transpose(ps_t[:, o:o + 128], src, ident[:, :])
                        last.then_inc(vt_mm, 1)

                def scores(i, u):
                    hh, half, j = unit(u)
                    if u % 10 == 0:
                        pe.wait_ge(qs_ok, i * 2 + (QS0 + hh + 1))
                        pe.wait_ge(kl_ok, i * 2 + (KL0 + hh + 1))
                    pe.wait_ge(p_exp, i * U + (EX0 + u - 1))
                    out = ps_s[u % 2]
                    if half is None:
                        q = qh[:, hh, LS + 128 * j:LS + 128 * j + 128]
                        for n, k in enumerate((kh, kl)):
                            last = pe.matmul(out[:, 512:768], q, k[:, hh, LS + 256:1536], start=n == 0, stop=n == 1)
                    else:
                        q = qh[:, hh, 256 * j + 128 * half:256 * j + 128 * half + 128]
                        loc = out[:, 0:384].rearrange("p (r c) -> p r c", c=32)
                        pe.matmul(out[:, 0:384], ident_b[:, :], mask[:, 3 * half + BIAS_T[j], :], start=True, stop=False)
                        for n, k in enumerate((kh, kl)):
                            pe.matmul(loc, q, grid(k[:, hh, 0:LS], 4 * half, 12, BANDS[j], 32), start=False, stop=n == 1)
                        for n, k in enumerate((kh, kl)):
                            last = pe.matmul(out[:, 512:768], q, k[:, hh, LS:LS + 256], start=n == 0, stop=n == 1)
                    last.then_inc(s_mm, 1)

                def start(i):
                    pe.wait_ge(mk_ok, 3)
                    scores(i, 0)
                    scores(i, 1)

                def blocks(u):
                    hh, half, j = unit(u)
                    if half is None:
                        return [(3, 18), (4, 19)]
                    return [(b, 4 * j + half + b) for b in range(3)] + [(3, 16), (4, 17)]

                def steps(i, u):
                    if u + 2 < U:
                        scores(i, u + 2)
                    if u < U:
                        pe.wait_ge(pn_ok, i * U + (u + 1))
                        pe.wait_ge(ptl_ok, i * U + (PTL0 + u))
                        for b, _ in blocks(u):
                            last = pe.transpose(ps_t[:, 128 * b:128 * b + 128], pb[:, u % 3, 128 * b:128 * b + 128],
                                                ident[:, :])
                        last.then_inc(t_mm, 1)
                    if u >= 1:
                        v = u - 1
                        pe.wait_ge(ptl_ok, i * U + (PTL0 + v + 1))
                        pe.wait_ge(ol_ok, i * U + (OL0 + v - 1))
                        if v == 0:
                            pe.wait_ge(vr_ok, i * 6 + 6)
                        prods = [(vt, b, vw, px) for b, vt in blocks(v)
                                 for vw, px in ((vh, pth), (vh, ptl), (vl, pth))]
                        for n, (vt, b, vw, px) in enumerate(prods):
                            last = pe.matmul(ps_o[v % 2][:, 0:128], vw[:, vt, :], px[:, v % 2, b, :],
                                             start=n == 0, stop=n == len(prods) - 1)
                        last.then_inc(pv_mm, 1)
                run(pe, per_pair, start, lambda i, hh: None, steps)

            @block.scalar
            def _(act):
                act.sem_inc(p_exp, EX0)
                act.activation(ident_b[:, :], ident[:, :], ACT.Copy).then_inc(mk_ok, 1)
                for n in range(2):
                    act.wait_ge(m_in, 16 * n + 16)
                    act.activation(mask[:, :, :].rearrange("p a b -> p (a b)")[:, 1152 * n:1152 * n + 1152],
                                   pb[:, :, :].rearrange("p a b -> p (a b)")[:, 0:1152], ACT.Copy).then_inc(mk_ok, 1)

                def per_pair(i):
                    act.wait_ge(pv_mm, i * U + PV0)
                    for r, (b0, b1) in enumerate(ROUNDS):
                        act.wait_ge(vt_mm, i * 5 + (r + 1))
                        o = (r % 2) * 512
                        act.activation(vh[:, b0:b1, :], ps_t[:, o:o + 128 * (b1 - b0)].rearrange(
                            "p (b n) -> p b n", n=128), ACT.Copy).then_inc(vh_ok, 1)
                    act.activation(vh[:, 16:18, :], kr[:, V_CACHE:2560].rearrange("p (b n) -> p b n", n=128),
                                   ACT.Copy).then_inc(vh_ok, 1)

                def head(i, hh):
                    act.wait_ge(s_mm, i * U + (10 * hh + 10))
                    act.wait_ge(qr_in, i * 64 + (32 * hh + 32))
                    act.activation(blocked(qh[:, hh, 0:LS]), qr[:, 0:LS].rearrange("p (r j c) -> p r j c", j=4, c=16),
                                   ACT.Copy, scale=HD ** -0.5)
                    act.activation(qh[:, hh, LS:TOK], qr[:, LS:TOK], ACT.Copy, scale=HD ** -0.5).then_inc(qh_ok, 1)
                    act.wait_ge(kr_in, i * 288 + (96 * hh + 192))
                    act.activation(kh[:, hh, :], kr[:, 0:1536], ACT.Copy).then_inc(kh_ok, 1)

                def exps(i, u):
                    _, half, _ = unit(u)
                    p, q = pb[:, u % 3, :], stat[:, u % 3, :]
                    act.wait_ge(nm_ok, i * U + (NM0 + u + 1))
                    if half is not None:
                        act.activation(p[:, 0:384], p[:, 0:384], ACT.Exp, bias=q[:, 2:3], accum_out=q[:, 3:4])
                    act.activation(p[:, 384:640], ps_s[u % 2][:, 512:768], ACT.Exp, bias=q[:, 2:3],
                                   accum_out=q[:, 4:5]).then_inc(p_exp, 1)

                def start(i):
                    exps(i, 0)
                    exps(i, 1)

                def steps(i, u):
                    if u < U:
                        c0 = 0 if unit(u)[1] is not None else 3
                        act.wait_ge(t_mm, i * U + (T0 + u + 1))
                        act.wait_ge(pv_mm, i * U + (PV0 + u - 1))
                        act.activation(pth[:, u % 2, c0:5, :], ps_t[:, 128 * c0:640].rearrange(
                            "p (b n) -> p b n", n=128), ACT.Copy).then_inc(pth_ok, 1)
                    if u + 2 < U:
                        exps(i, u + 2)
                    if u >= 1:
                        act.wait_ge(pv_mm, i * U + (PV0 + u))
                        rows, dst = out_view(a_h, i, u - 1)
                        act.activation(dst, src_view(rows, u - 1), ACT.Copy).then_inc(oh_ok, 1)
                run(act, per_pair, start, head, steps)

            @block.gpsimd
            def _(pool):
                pool.sem_inc(kl_ok, KL0)

                def head(i, hh):
                    pool.wait_ge(kh_ok, i * 2 + (hh + 1))
                    pool.tensor_tensor(kl[:, hh, :], kr[:, 0:1536], kh[:, hh, :].bitcast(F32), ALU.subtract).then_inc(kl_ok, 1)

                def norm(i, u):
                    c0 = 0 if unit(u)[1] is not None else 384
                    pool.wait_ge(rr_ok, i * U + (u + 1))
                    pool.sem_inc(turn, 1)
                    pool.tensor_scalar(pb[:, u % 3, c0:640], pb[:, u % 3, c0:640], stat[:, u % 3, 6:7], 1.0,
                                       ALU.mult, ALU.mult).then_inc(pn_ok, 1)

                def start(i):
                    norm(i, 0)
                    norm(i, 1)

                def steps(i, u):
                    if u + 2 < U:
                        norm(i, u + 2)
                run(pool, None, start, head, steps)

            @block.vector
            def _(dve):
                dve.sem_inc(qs_ok, QS0)
                dve.sem_inc(nm_ok, NM0)
                dve.sem_inc(ptl_ok, PTL0)
                dve.sem_inc(ol_ok, OL0)

                def per_pair(i):
                    for r, (b0, b1) in enumerate(ROUNDS):
                        dve.wait_ge(vh_ok, i * 6 + (r + 1))
                        o = (r % 2) * 512
                        dve.tensor_tensor(vl[:, b0:b1, :], ps_t[:, o:o + 128 * (b1 - b0)].rearrange(
                            "p (b n) -> p b n", n=128), vh[:, b0:b1, :].bitcast(F32), ALU.subtract).then_inc(vr_ok, 1)
                    dve.wait_ge(vh_ok, i * 6 + 6)
                    dve.tensor_tensor(vl[:, 16:18, :], kr[:, V_CACHE:2560].rearrange("p (b n) -> p b n", n=128),
                                      vh[:, 16:18, :].bitcast(F32), ALU.subtract).then_inc(vr_ok, 1)

                def head(i, hh):
                    dve.wait_ge(qh_ok, i * 2 + (hh + 1))
                    lo = qh[64:128, hh, :]
                    for j in range(4):
                        b = lo[:, 256 * j:256 * j + 256].rearrange("p (r c) -> p r c", c=16)
                        dve.scalar_tensor_tensor(b, grid(qr[64:128, 0:LS], 0, 16, 16 * j, 16), HD ** -0.5, b.bitcast(F32),
                                                 ALU.mult, ALU.subtract)
                    dve.scalar_tensor_tensor(lo[:, LS:TOK], qr[64:128, LS:TOK], HD ** -0.5, lo[:, LS:TOK].bitcast(F32),
                                             ALU.mult, ALU.subtract).then_inc(qs_ok, 1)

                def maxima(i, u):
                    hh, half, j = unit(u)
                    q, out = stat[:, u % 3, :], ps_s[u % 2]
                    dve.wait_ge(s_mm, i * U + (S0 + u + 1))
                    dve.wait_ge(t_mm, i * U + (T0 + u - 2))
                    if half is not None:
                        if u % 10 == 0:
                            dve.wait_ge(b_in[hh], i * 128 + 128)
                        x = BIAS_X[j]
                        dve.sem_inc(turn_v, 1)
                        dve.tensor_tensor_reduce(
                            out=pb[:, u % 3, 0:384].rearrange("p (r c) -> p r c", c=32),
                            in0=out[:, 0:384].rearrange("p (r c) -> p r c", c=32),
                            in1=backwards(bias[:, hh, 4 * half:4 * half + 12, 31 - x:63 - x]), scale=1.0, scalar=-3.0e38,
                            op0=ALU.add, op1=ALU.max, accum_out=q[:, 0:1])
                    dve.reduce_max(q[:, 1:2], out[:, 512:768], AX.X).then_inc(mx_ok, 1)
                    dve.wait_ge(mx_ok, i * U + (u + 1))
                    if half is not None:
                        ins = dve.tensor_scalar(q[:, 2:3], q[:, 0:1], q[:, 1:2], -1.0, ALU.max, ALU.mult)
                    else:
                        ins = dve.tensor_scalar(q[:, 2:3], q[:, 1:2], -1.0, None, ALU.mult)
                    ins.then_inc(nm_ok, 1)

                def recip(i, u):
                    q = stat[:, u % 3, :]
                    dve.wait_ge(p_exp, i * U + (EX0 + u + 1))
                    if unit(u)[1] is not None:
                        dve.tensor_tensor(q[:, 5:6], q[:, 3:4], q[:, 4:5], ALU.add).then_inc(tot_ok, 1)
                    else:
                        dve.tensor_copy(q[:, 5:6], q[:, 4:5]).then_inc(tot_ok, 1)
                    dve.wait_ge(tot_ok, i * U + (u + 1))
                    dve.reciprocal(q[:, 6:7], q[:, 5:6]).then_inc(rr_ok, 1)

                def start(i):
                    for u in range(2):
                        maxima(i, u)
                        recip(i, u)

                def steps(i, u):
                    if u + 2 < U:
                        maxima(i, u + 2)
                    if u < U:
                        c0 = 0 if unit(u)[1] is not None else 3
                        dve.wait_ge(pth_ok, i * U + (u + 1))
                        dve.tensor_tensor(ptl[:, u % 2, c0:5, :], ps_t[:, 128 * c0:640].rearrange(
                            "p (b n) -> p b n", n=128), pth[:, u % 2, c0:5, :].bitcast(F32),
                            ALU.subtract).then_inc(ptl_ok, 1)
                    if u + 2 < U:
                        recip(i, u + 2)
                    if u >= 1:
                        dve.wait_ge(oh_ok, i * U + u)
                        rows, dst = out_view(a_l, i, u - 1)
                        hi = out_view(a_h, i, u - 1)[1]
                        dve.tensor_tensor(dst, src_view(rows, u - 1), hi.bitcast(F32), ALU.subtract).then_inc(ol_ok, 1)
                run(dve, per_pair, start, head, steps)

        e0 = layer_rest(1, e0)
        assert e0 - wsh == t["w_all"].shape[0], (e0 - wsh, t["w_all"].shape)


def host_layout(inputs):
    f = np.float32
    g = {k: np.asarray(v) for k, v in inputs.items()}
    out = {}

    def cols(v):
        return v.reshape(-1, 128).T

    def entry(w):
        return w.reshape(-1, 128, 128).transpose(1, 0, 2).reshape(128, -1)

    def basis(b):
        e = np.zeros((128, 1024), f)
        x = entry(b.astype(f))
        e[:, :x.shape[1]] = x
        return e

    out["x"] = np.concatenate([g["x_sample"][0], g["x_prompt"][0]], 0).T.reshape(KT, 128, TOK)
    out["cvec"] = np.stack([g["c"][0], g["c_ctx"]], -1).reshape(8, 128, 2).transpose(1, 0, 2)
    conv = np.concatenate([g["hy_sconv_w"][0], g["hy_sconv_b"]], 0).reshape(4, 3, 8, 128)[:, [1, 2, 0]]
    conv = conv.transpose(3, 2, 1, 0).reshape(128, 96)
    ln = np.stack([g[n][l] for l in range(2) for n in ("ln1_g", "ln1_b", "ln2_g", "ln2_b")]).reshape(8, 8, 128)
    out["par"] = np.concatenate([conv, ln.transpose(2, 0, 1).reshape(128, 64), cols(g["hy_bias"][0]),
                                 cols(g["ada_b"].reshape(-1))], 1)
    out["ident"] = np.eye(128, dtype=f)
    out["ada"] = g["ada_w"].reshape(2, 8, 128, 48, 128).transpose(0, 3, 2, 1, 4).reshape(96, 128, 1024)
    out["pe_w1"], out["pe_w2"] = g["hy_pe_w1"][0], g["hy_pe_w2"][0]
    out["fcol"] = np.stack([g["hy_pe_b1"][0], g["hy_pe_b2"][0], g["hy_sin_freq"][0, 0], g["hy_sin_freq"][0, 1]], 1)
    out["pe_w3"] = g["hy_pe_w3"][0].reshape(FILT, 2, 2, 512).transpose(2, 0, 1, 3)
    out["dec"] = np.broadcast_to(g["hy_decay"][0].reshape(2, 2, 512).transpose(1, 0, 2)[:, None], (2, 128, 2, 512))
    feats, negt = [], []
    for n in (LS, LP):
        order = np.concatenate([np.arange(0, n, 2), np.arange(1, n, 2)])
        tt = np.linspace(0.0, 1.0, n, dtype=f)[:, None]
        w = (f(2.0 * math.pi / n) * np.arange(n, dtype=f))[:, None]
        bands = np.linspace(1e-4, 15, 16, dtype=f)[None, :]
        feats.append(np.concatenate([tt, np.cos(bands * w), np.sin(bands * w)], -1)[order].T)
        negt.append(cols(-tt[order, 0]))
    out["feats"], out["negt"] = np.concatenate(feats, 1), np.concatenate(negt, 1)

    a_tiles = [np.arange(0, 256, 2), np.arange(1, 256, 2), np.arange(256, 512, 2), np.arange(257, 512, 2)]
    freq = a_tiles + [LS - 1 - a_tiles[a ^ 1] for a in range(4)]
    freq_p = [np.arange(128), LP - 1 - np.arange(128)]

    def angle(n, m, length):
        return np.outer(n, np.pi * (2 * m + 1) / (2 * length))

    filt = []
    for a in range(4):
        for fn in (np.cos, np.sin):
            n = np.concatenate([np.arange(0, LS, 2), np.arange(1, LS, 2)])
            filt.append(basis(fn(angle(n, freq[a], LS))))
    for fn in (np.cos, np.sin):
        n = np.concatenate([np.arange(0, LP, 2), np.arange(1, LP, 2)])
        filt.append(basis(fn(angle(n, freq_p[0], LP))))
    fwd = []
    for m in freq:
        x = angle(np.arange(LS // 2) + 0.5, m, LS)
        fwd.append(basis(np.concatenate([np.cos(x) + np.sin(x), np.cos(x) - np.sin(x)])))
    blocks = []
    for m in freq_p:
        x = angle(np.arange(LP // 2) + 0.5, m, LP)
        cas, cms, even = np.cos(x) + np.sin(x), np.cos(x) - np.sin(x), (m % 2 == 0)[None]
        blocks += [cas * even, cas * ~even, cms * ~even, cms * even]
    fwd.append(basis(np.concatenate(blocks)))
    inv = []
    for m in freq:
        x = angle(np.arange(LS // 2) + 0.5, m, LS).T
        inv += [np.cos(x) + np.sin(x), np.cos(x) - np.sin(x)]
    out["inv"] = (np.stack(inv, 1) / (2 * LS)).astype(f).reshape(128, 4, 2048).transpose(1, 0, 2)
    inv = []
    for m in freq_p:
        x = angle(np.arange(LP) + 0.5, m, LP).T
        inv += [np.cos(x) + np.sin(x), np.cos(x) - np.sin(x)]
    out["inv_p"] = (np.stack(inv, 1) / (2 * LP)).astype(f).reshape(128, 1024)

    def tiles(w):
        return w.reshape(8, 128, -1, 128).transpose(2, 1, 0, 3).reshape(-1, 128, 1024)

    w_in = tiles(g["hy_w_in"][0]).reshape(3, 8, 128, 1024)[[1, 2, 0]].transpose(1, 0, 2, 3).reshape(24, 128, 1024)

    def ffn(l):
        inn = tiles(g["ffn_w_in"][l]).reshape(2, FC, 2, 128, 1024).transpose(1, 2, 0, 3, 4).reshape(FC, 4, 128, 1024)
        o = g["ffn_w_out"][l].reshape(FC, 2, 128, 2, 4, 128).transpose(0, 3, 2, 4, 1, 5).reshape(FC, 2, 128, 1024)
        seq = [inn[0]]
        for i in range(1, FC):
            seq += [inn[i], o[i - 1]]
        return np.concatenate(seq + [o[FC - 1]])

    out["w_all"] = np.concatenate([np.stack(filt), np.stack(filt), w_in, np.stack(fwd), tiles(g["hy_w_out"][0]), ffn(0),
                                   tiles(g["na_w_qkv"][0]), tiles(g["na_w_out"][0]), ffn(1)])
    ck = g["cache_k"][0, 0]
    out["cache_kt"] = ck.transpose(0, 2, 1)
    out["cache_v"] = g["cache_v"][0, 0].reshape(8, 2, 2, 128, 64).transpose(0, 3, 2, 1, 4).reshape(8, 128, 2, 128)
    rpb = np.zeros((NH, RPB_H * RPB_W + RPB_W), f)
    rpb[:, :RPB_H * RPB_W].reshape(NH, RPB_H, RPB_W)[:, 4:19, 16:47] = g["na_rpb"][0]
    out["rpb"] = rpb[:, ::-1]
    mask = np.zeros((2, 3, 8, 16, 12, 32), f)
    for half in range(2):
        for j in (0, 1, 3):
            for r in range(8):
                row0 = min(max(8 * half + r - 4, 0), 8) - 4 * half
                for c in range(16):
                    col0 = min(max(16 * j + c - 8, 0), 48) - BANDS[j]
                    m = np.full((12, 32), MASKED, f)
                    m[row0:row0 + 8, col0:col0 + 16] = 0
                    mask[half, BIAS_T[j], r, c] = m
    out["mask"] = mask.reshape(2, 3, 128, 384).transpose(2, 0, 1, 3).reshape(128, 6, 384)
    return {k: np.ascontiguousarray(v, dtype=f) for k, v in out.items()}


def kernel(**inputs):
    import concourse.bacc as bacc
    from concourse.bass_utils import run_bass_kernel_spmd
    nc = bacc.Bacc("TRN2", target_bir_lowering=False, num_devices=1)
    arrays = host_layout(inputs)
    t = {k: nc.dram_tensor("in_" + k, v.shape, F32, kind="ExternalInput").ap() for k, v in arrays.items()}
    outs = {"y": (KT, 128, TOK), "nk": (8, 128, LP), "nv": (8, 128, LP)}
    for k, s in outs.items():
        t[k] = nc.dram_tensor("out_" + k, s, F32, kind="ExternalOutput").ap()
    hyena_natten_step(nc, t)
    r = run_bass_kernel_spmd(nc, [{"in_" + k: v for k, v in arrays.items()}], core_ids=[0]).results[0]
    y = r["out_y"].reshape(D, TOK).T
    kv = [r[n].reshape(1, 1, NH, HD, LP).transpose(0, 1, 2, 4, 3) for n in ("out_nk", "out_nv")]
    return (np.ascontiguousarray(y[LS:][None]), np.ascontiguousarray(y[:LS][None]),
            np.ascontiguousarray(kv[0]), np.ascontiguousarray(kv[1]))
```

```python
import concourse.bass as bass
from concourse import mybir
from contextlib import ExitStack
import math
import numpy as np

F32 = mybir.dt.float32
F32R = mybir.dt.float32r
BF16 = mybir.dt.bfloat16
ALU = mybir.AluOpType
ACT = mybir.ActivationFunctionType
AX = mybir.AxisListType

D = 1024
KT = D // 128
LS, LP = 1024, 256
TOK = LS + LP
CHUNKS = ((0, 512), (512, 1024), (1024, TOK))
PARTS = ((0, LS), (LS, TOK))
DFF = 2816
FC = DFF // 256
NH, HD = 16, 64
GW = 64
ALPHA = (2 * 2) ** 0.25
EPS = 1e-5
FILT, PE_DIM = 64, 33
TWO_PI_HI = 6.28125
TWO_PI_LO = 2 * math.pi - TWO_PI_HI
MAGIC = 12582912.0
MASKED = -1e30
RPB_H, RPB_W = 23, 63
BANDS = (0, 8, 24, 32)
BIAS_X = (16, 8, 8, 0)
BIAS_T = (0, 1, 1, 2)
SH1, SC1, G1, SH2, SC2, G2 = range(6)

E_FILT, E_IN, E_FWD, E_INV, E_OUT, E_FFN, E_QKV = 20, 24, 9, 24, 8, 6 * FC, 24


def hyena_natten_step(nc, t):
    ctx = ExitStack()
    with ctx:
        names = [0]

        def sb(name, shape, dt=F32, where=ctx):
            names[0] += 1
            return where.enter_context(nc.sbuf_tensor(f"{name}_{names[0]}", shape, dt))

        def sem(name, where=ctx):
            names[0] += 1
            if where is ctx:
                return ctx.enter_context(nc.semaphore(f"{name}_{names[0]}"))
            handle = nc.alloc_semaphore(f"{name}_{names[0]}")
            stage_sems.append(handle)
            return handle

        stage_sems = []

        def clear():
            nc.clear_and_free_semaphores(stage_sems)
            stage_sems.clear()
            nc.all_engine_barrier()

        def stage():
            st = ExitStack()
            st.callback(clear)
            return st


        raw = sb("w_raw", [128, 2, 1024])
        wh = sb("w_hi", [128, 2, 1024], F32R)
        wl = sb("w_lo", [128, 2, 1024], F32R)
        ident = sb("ident", [128, 128])
        meanw = sb("meanw", [128, 128])
        par = sb("par", [128, 264])
        conv_p = par[:, 0:96].rearrange("p (t n) -> p t n", n=4)
        ln_p = par[:, 96:160].rearrange("p (s k) -> p s k", k=8)
        hb_p = par[:, 160:168]
        adab = par[:, 168:264]
        mod = sb("mod", [128, 96, 2])
        silc = sb("silc", [128, 8, 2])
        aff = sb("aff", [128, 2, 8, 2])
        axs = sb("axs", [128, 2, 8])
        eps = sb("eps", [128, 1])
        a_h = sb("a_hi", [128, KT, TOK], F32R)
        a_l = sb("a_lo", [128, KT, TOK], F32R)

        def dram(name, shape):
            return nc.dram_tensor(name, shape, F32).ap()
        spec = dram("spec", (10, 128, 2, D))
        x0_d = dram("x0_d", (KT, 128, TOK))
        s_d = dram("s_d", (KT, 128, TOK))
        y_d = dram("y_d", (KT, 3, 128, 8, 128))
        qkv_d = dram("qkv_d", (24, 128, TOK))
        x_d = dram("x_d", (KT, 128, TOK))

        w_loaded = [sem("w_loaded0"), sem("w_loaded1")]
        w_hi, w_split, w_used = sem("w_hi"), sem("w_split"), sem("w_used")

        def at(c, i=None, n=0):
            return c if i is None or n == 0 else i * n + c

        def load_entry(sp, c, src, i=None, n=0, width=1024):
            if c >= 2:
                sp.wait_ge(w_split, at(c - 1, i, n))
            sp.dma_start(raw[:, c % 2, 0:width], src).then_inc(w_loaded[c % 2], 16)

        def split_hi(act, c, i=None, n=0, width=1024):
            s = c % 2
            act.wait_ge(w_loaded[s], at(16 * (c // 2) + 16, i, 8 * n))
            if c >= 2:
                act.wait_ge(w_used, at(c - 1, i, n))
            act.activation(wh[:, s, 0:width], raw[:, s, 0:width], ACT.Copy).then_inc(w_hi, 1)

        def split_lo(pool, c, i=None, n=0, width=1024):
            s = c % 2
            pool.wait_ge(w_hi, at(c + 1, i, n))
            pool.tensor_tensor(wl[:, s, 0:width], raw[:, s, 0:width], wh[:, s, 0:width].bitcast(F32),
                               ALU.subtract).then_inc(w_split, 1)

        def products(pe, c, blocks, chunks, start=True, stop=True):
            for b, (blk, xh, xl, out) in enumerate(blocks):
                for term, (w, x) in enumerate(((wh, xh), (wh, xl), (wl, xh))):
                    for c0, c1 in chunks:
                        last = pe.matmul(out[:, c0:c1], w[:, c % 2, blk * 128:blk * 128 + 128], x[:, c0:c1],
                                         start=start and b == 0 and term == 0,
                                         stop=stop and b == len(blocks) - 1 and term == 2)
            return last

        def wsrc(w):
            return t["w_all"][w, :, :]

        fst = ExitStack()
        hd2 = sb("hd2", [FILT, TOK], F32, fst)
        hdb = sb("hdb", [FILT, 2, 128], F32, fst)
        negt = sb("negt", [128, 10], F32, fst)
        with stage() as st:
            cvec = sb("cvec", [128, 8, 2], F32, st)
            feats = sb("feats", [PE_DIM, TOK], F32, st)
            w1 = sb("pe_w1", [PE_DIM, FILT], F32, st)
            w2 = sb("pe_w2", [FILT, FILT], F32, st)
            fcol = sb("fcol", [FILT, 4], F32, st)
            arg = sb("arg", [FILT, TOK], F32, st)
            cyc = sb("cyc", [FILT, TOK], F32, st)
            hd = sb("hd", [FILT, TOK], F32, st)
            ps_mlp = st.enter_context(nc.psum_tensor("ps_mlp", [128, 1536], F32))
            c_in = sem("c_in", st)
            mlp_mm, arg_ok, dve_s, hd_ok, clr = sem("mlp_mm", st), sem("arg_ok", st), sem("dve_s", st), sem("hd_ok", st), sem("clr", st)
            block = st.enter_context(nc.Block())

            @block.sync
            def _(sp):
                for dst, src in ((cvec[:, :, :], t["cvec"]), (par[:, :], t["par"]), (ident[:, :], t["ident"]),
                                 (feats[:, :], t["feats"]), (w1[:, :], t["pe_w1"]), (w2[:, :], t["pe_w2"]),
                                 (fcol[:, :], t["fcol"]), (negt[:, :], t["negt"])):
                    sp.dma_start(dst, src).then_inc(c_in, 16)
                load_entry(sp, 0, wsrc(0))
                load_entry(sp, 1, wsrc(1))

            @block.gpsimd
            def _(pool):
                pool.memset(meanw[:, :], 1.0 / D)
                pool.memset(eps[:, :], EPS)
                split_lo(pool, 0)
                split_lo(pool, 1)

            @block.scalar
            def _(act):
                act.wait_ge(c_in, 128)
                act.activation(silc[:, :, :], cvec[:, :, :], ACT.Silu)
                split_hi(act, 0)
                split_hi(act, 1)
                act.wait_ge(arg_ok, 1)
                act.activation(hd[:, :], arg[:, :], ACT.Sin).then_inc(hd_ok, 1)
                act.wait_ge(arg_ok, 2)
                act.activation(hd2[:, :], arg[:, :], ACT.Sin).then_inc(hd_ok, 1)
                act.wait_ge(hd_ok, 2)
                act.activation(hdb[:, 0, :], hd2[:, 0:128], ACT.Copy).then_inc(hd_ok, 1)
                act.activation(hdb[:, 1, :], hd2[:, LS:LS + 128], ACT.Copy).then_inc(hd_ok, 1)

            @block.vector
            def _(dve):
                dve.wait_ge(c_in, 128)
                for layer, (b, q) in enumerate(((0, 2), (1, 3))):
                    dve.wait_ge(mlp_mm, layer + 1)
                    dve.tensor_scalar(arg[:, :], ps_mlp[0:FILT, 0:TOK], fcol[:, b:b + 1],
                                      fcol[:, q:q + 1], ALU.add, ALU.mult).then_inc(dve_s, 1)
                    dve.wait_ge(dve_s, 5 * layer + 1)
                    dve.tensor_scalar(cyc[:, :], arg[:, :], 1.0 / (2 * math.pi), MAGIC, ALU.mult,
                                      ALU.add).then_inc(dve_s, 1)
                    dve.wait_ge(dve_s, 5 * layer + 2)
                    dve.tensor_scalar(cyc[:, :], cyc[:, :], MAGIC, None, ALU.subtract).then_inc(dve_s, 1)
                    dve.wait_ge(dve_s, 5 * layer + 3)
                    dve.scalar_tensor_tensor(arg[:, :], cyc[:, :], -TWO_PI_HI, arg[:, :], ALU.mult,
                                             ALU.add).then_inc(dve_s, 1)
                    dve.wait_ge(dve_s, 5 * layer + 4)
                    dve.scalar_tensor_tensor(arg[:, :], cyc[:, :], -TWO_PI_LO, arg[:, :], ALU.mult,
                                             ALU.add).then_inc(dve_s, 1)
                    dve.wait_ge(dve_s, 5 * layer + 5)
                    dve.tensor_scalar(arg[:, :], arg[:, :], 3.1415925, -3.1415925, ALU.min,
                                      ALU.max).then_inc(arg_ok, 1)
                dve.wait_ge(hd_ok, 4)
                dve.memset(hdb[:, :, 0:1], 0.0)

            @block.tensor
            def _(pe):
                pe.wait_ge(c_in, 128)
                for c0, c1 in CHUNKS:
                    last = pe.matmul(ps_mlp[0:FILT, c0:c1], w1[:, :], feats[:, c0:c1], start=True, stop=True)
                last.then_inc(mlp_mm, 1)
                pe.wait_ge(hd_ok, 1)
                for c0, c1 in CHUNKS:
                    last = pe.matmul(ps_mlp[0:FILT, c0:c1], w2[:, :], hd[:, c0:c1], start=True, stop=True)
                last.then_inc(mlp_mm, 1)

        e0 = 0
        with stage() as st:
            w3 = sb("pe_w3", [FILT, 2, 512], F32, st)
            dec = sb("dec", [128, 2, 512], F32, st)
            win = sb("win", [128, 2, 2, 512], F32, st)
            ker = sb("ker", [128, 2, 2, 512], F32, st)
            pq = sb("pq", [128, 2, 2, 512], F32, st)
            pqh = sb("pq_hi", [128, 10, 2, 512], F32R, st)
            pql = a_l[:, :, :].rearrange("p k t -> p (k t)")[:, 0:10240].rearrange("p (n s c) -> p n s c", n=10, s=2)
            odd = sb("odd", [128, 2, 512], F32, st)
            gout = sb("gout", [128, 2, 2, 512], F32, st)
            awr = sb("ada_raw0", [128, 2, 1024], F32, st)
            ps = [st.enter_context(nc.psum_tensor(f"ps_f{b}", [128, 512], F32)) for b in range(8)]
            f_w, dec_ok, pe_k, win_ok, ker_ok, pq_ok, ph_ok, pl_ok = [
                sem(n, st) for n in ("f_w", "dec_ok", "pe_k", "win_ok", "ker_ok", "pq_ok", "ph_ok", "pl_ok")]
            odd_ok, spec_ev, g_out = sem("odd_ok", st), sem("spec_ev", st), [sem("g_out0", st), sem("g_out1", st)]
            a_in, pe_a = [sem("a_in0", st), sem("a_in1", st)], sem("pe_a", st)
            block = st.enter_context(nc.Block())

            @block.sync
            def _(sp):
                sp.sem_inc(g_out[0], 1)
                sp.sem_inc(g_out[1], 1)
                for n in range(2):
                    sp.dma_start(awr[:, n, :], t["ada"][n, :, :]).then_inc(a_in[n], 16)
                with sp.Fori(0, 2) as i:
                    load_entry(sp, e0 + 2, wsrc(i * 10 + (e0 + 2)), i, 10)
                    for j in range(10):
                        if j < 9:
                            load_entry(sp, e0 + 3 + j, wsrc(i * 10 + (e0 + 3 + j)), i, 10)
                        sp.wait_ge(spec_ev, 1 + i * 10 + (j + 1))
                        a = j // 2
                        for side, tile in enumerate((a, 4 + (a ^ 1)) if j < 8 else (8, 9)):
                            sp.dma_start(spec[tile, :, j % 2, bass.ds(i * 512, 512)],
                                         gout[:, j % 2, side, :]).then_inc(g_out[j % 2], 16)
                        if j < 8:
                            sp.wait_ge(pe_a, i * 8 + (j + 1))
                            sp.dma_start(awr[:, j % 2, :], t["ada"][i * 8 + (j + 2), :, :]).then_inc(a_in[j % 2], 16)
                for s in range(2):
                    sp.wait_ge(g_out[s], 321)
                    sp.wait_ge(a_in[s], 144)

            @block.gpsimd
            def _(pool):
                with pool.Fori(0, 2) as i:
                    for n in range(10):
                        pool.wait_ge(ph_ok, i * 10 + (n + 1))
                        pool.tensor_tensor(pql[:, n, :, :], pq[:, n % 2, :, :], pqh[:, n, :, :].bitcast(F32),
                                           ALU.subtract).then_inc(pl_ok, 1)
                    for j in range(10):
                        split_lo(pool, e0 + 2 + j, i, 10)

            @block.scalar
            def _(act):
                with act.Fori(0, 2) as i:
                    act.dma_start(dec[:, :, :], t["dec"][i, :, :, :]).then_inc(f_w, 16)
                    act.dma_start(w3[:, :, :], t["pe_w3"][i, :, :, :]).then_inc(f_w, 16)
                    act.wait_ge(f_w, i * 32 + 32)
                    act.activation(dec[:, :, :], dec[:, :, :], ACT.Abs).then_inc(dec_ok, 1)
                    act.wait_ge(dec_ok, i + 1)
                    for n in range(11):
                        if n < 10:
                            if n >= 2:
                                act.wait_ge(ker_ok, i * 10 + (n - 1))
                            act.activation(win[:, n % 2, :, :], dec[:, :, :], ACT.Exp,
                                           scale=negt[:, n:n + 1]).then_inc(win_ok, 1)
                        if n >= 1:
                            act.wait_ge(pq_ok, i * 10 + n)
                            act.activation(pqh[:, n - 1, :, :], pq[:, (n - 1) % 2, :, :],
                                           ACT.Copy).then_inc(ph_ok, 1)
                    for j in range(10):
                        act.wait_ge(w_used, i * 10 + (e0 + j + 1))
                        split_hi(act, e0 + 2 + j, i, 10)
                        if j >= 2:
                            act.wait_ge(spec_ev, 1 + i * 10 + (j - 1))
                        act.activation(odd[:, j % 2, :], ps[2 * (j % 3) + 1][:, :], ACT.Copy).then_inc(odd_ok, 1)

            @block.vector
            def _(dve):
                dve.sem_inc(spec_ev, 1)
                with dve.Fori(0, 2) as i:
                    for n in range(10):
                        dve.wait_ge(win_ok, i * 10 + (n + 1))
                        dve.wait_ge(pe_k, i * 10 + (n + 1))
                        for side in range(2):
                            ins = dve.scalar_tensor_tensor(ker[:, n % 2, side, :], win[:, n % 2, side, :], 0.05,
                                                           ps[2 * (n % 2) + side][:, :], ALU.add, ALU.mult)
                        ins.then_inc(ker_ok, 1)
                        dve.wait_ge(ker_ok, i * 10 + (n + 1))
                        if n >= 2:
                            dve.wait_ge(pl_ok, i * 10 + (n - 1))
                        dve.tensor_tensor(pq[:, n % 2, 0, :], ker[:, n % 2, 0, :], ker[:, n % 2, 1, :], ALU.add)
                        dve.tensor_tensor(pq[:, n % 2, 1, :], ker[:, n % 2, 0, :], ker[:, n % 2, 1, :],
                                          ALU.subtract).then_inc(pq_ok, 1)
                    for j in range(10):
                        dve.wait_ge(g_out[j % 2], 1 + i * 160 + 32 * (j // 2))
                        dve.wait_ge(odd_ok, i * 10 + (j + 1))
                        even = ps[2 * (j % 3)]
                        dve.tensor_tensor(gout[:, j % 2, 0, :], even[:, :], odd[:, j % 2, :], ALU.add)
                        if j % 2 == 0:
                            ins = dve.tensor_tensor(gout[:, j % 2, 1, :], even[:, :], odd[:, j % 2, :], ALU.subtract)
                        else:
                            ins = dve.scalar_tensor_tensor(gout[:, j % 2, 1, :], even[:, :], -1.0,
                                                           odd[:, j % 2, :], ALU.mult, ALU.add)
                        ins.then_inc(spec_ev, 1)
                dve.wait_ge(pe_a, 16)
                dve.tensor_tensor(mod[:, 0:16, :], ps[7][:, 0:32].rearrange("p (a b) -> p a b", b=2),
                                  adab[:, 0:16].unsqueeze(2).to_broadcast([128, 16, 2]), ALU.add)

            @block.tensor
            def _(pe):
                with pe.Fori(0, 2) as i:
                    pe.wait_ge(spec_ev, 1 + i * 10)
                    pe.wait_ge(f_w, i * 32 + 32)
                    for n in range(10):
                        if n >= 2:
                            pe.wait_ge(ker_ok, i * 10 + (n - 1))
                        fwd = hd2[:, n * 128:n * 128 + 128]
                        bwd = hdb[:, n // 8, :] if n in (0, 8) else fwd
                        pe.matmul(ps[2 * (n % 2)][:, :], fwd, w3[:, 0, :], start=True, stop=True)
                        pe.matmul(ps[2 * (n % 2) + 1][:, :], bwd, w3[:, 1, :], start=True, stop=True).then_inc(pe_k, 1)
                    pe.wait_ge(pl_ok, i * 10 + 10)
                    for j in range(10):
                        pe.wait_ge(w_split, i * 10 + (e0 + j + 1))
                        if j >= 3:
                            pe.wait_ge(spec_ev, 1 + i * 10 + (j - 2))
                        even, od = ps[2 * (j % 3)], ps[2 * (j % 3) + 1]
                        taps = range(4) if j < 8 else range(1)
                        base = (0, 4) if j < 8 else (8, 9)
                        for side, out in enumerate((even, od)):
                            last = products(pe, e0 + j, [
                                (side * len(taps) + k, pqh[:, base[side] + k, j % 2, :],
                                 pql[:, base[side] + k, j % 2, :], out) for k in taps], ((0, 512),))
                        last.then_inc(w_used, 1)
                        if j < 8:
                            pe.wait_ge(a_in[j % 2], i * 64 + (16 * (j // 2) + 16))
                            for k in range(8):
                                last = pe.matmul(ps[7][:, bass.ds(i * 16 + 2 * j, 2)], awr[:, j % 2, k * 128:k * 128 + 128],
                                                 silc[:, k, :], start=k == 0, stop=k == 7)
                            last.then_inc(pe_a, 1)
        fst.close()
        e0 += E_FILT

        def modulation(dve, done, layer, sc, sh, ln):
            m0 = layer * 48
            scale, shift = mod[:, m0 + sc * 8:m0 + sc * 8 + 8, :], mod[:, m0 + sh * 8:m0 + sh * 8 + 8, :]
            dve.tensor_scalar(aff[:, 0, :, :], scale, 1.0, None, ALU.add).then_inc(done, 1)
            dve.wait_ge(done, 1)
            if ln is None:
                dve.tensor_copy(aff[:, 1, :, :], shift).then_inc(done, 4)
            else:
                g = ln_p[:, ln, :].unsqueeze(2).to_broadcast([128, 8, 2])
                b = ln_p[:, ln + 1, :].unsqueeze(2).to_broadcast([128, 8, 2])
                dve.tensor_tensor(aff[:, 1, :, :], aff[:, 0, :, :], b, ALU.mult).then_inc(done, 1)
                dve.wait_ge(done, 2)
                dve.tensor_tensor(aff[:, 1, :, :], aff[:, 1, :, :], shift, ALU.add).then_inc(done, 1)
                dve.tensor_tensor(aff[:, 0, :, :], aff[:, 0, :, :], g, ALU.mult).then_inc(done, 1)
                dve.tensor_scalar(axs[:, :, :], ln_p[:, ln:ln + 2, :], ALPHA, None, ALU.mult).then_inc(done, 1)
            dve.wait_ge(done, 5)

        with stage() as st:
            xin = sb("xin", [128, KT, TOK], F32, st)
            xm = sb("xm", [128, 2, TOK], F32, st)
            x_in = [sem(f"x_in{k}", st) for k in range(KT)]
            coef, xm_ok, xh_ok, xl_ok, xl_v = [sem(n, st) for n in ("coef", "xm_ok", "xh_ok", "xl_ok", "xl_v")]
            block = st.enter_context(nc.Block())

            @block.sync
            def _(sp):
                for k in range(KT):
                    sp.dma_start(xin[:, k, :], t["x"][k, :, :]).then_inc(x_in[k], 16)

            @block.vector
            def _(dve):
                modulation(dve, coef, 0, SC1, SH1, None)
                for k in range(KT + 1):
                    if k < KT:
                        dve.wait_ge(x_in[k], 16)
                        if k >= 2:
                            dve.wait_ge((xl_ok, xl_v)[k % 2], k // 2)
                        for p, (p0, p1) in enumerate(PARTS):
                            ins = dve.tensor_scalar(xm[:, k % 2, p0:p1], xin[:, k, p0:p1], aff[:, 0, k, p:p + 1],
                                                    aff[:, 1, k, p:p + 1], ALU.mult, ALU.add)
                        ins.then_inc(xm_ok, 1)
                    if k % 2 == 0 and k:
                        dve.wait_ge(xm_ok, k)
                        dve.wait_ge(xh_ok, k)
                        dve.tensor_tensor(a_l[:, k - 1, :], xm[:, 1, :], a_h[:, k - 1, :].bitcast(F32),
                                          ALU.subtract).then_inc(xl_v, 1)

            @block.scalar
            def _(act):
                act.wait_ge(coef, 5)
                for k in range(KT):
                    act.wait_ge(x_in[k], 16)
                    for p, (p0, p1) in enumerate(PARTS):
                        ins = act.activation(a_h[:, k, p0:p1], xin[:, k, p0:p1], ACT.Identity,
                                             scale=aff[:, 0, k, p:p + 1], bias=aff[:, 1, k, p:p + 1])
                    ins.then_inc(xh_ok, 1)

            @block.gpsimd
            def _(pool):
                for k in range(0, KT, 2):
                    pool.wait_ge(xm_ok, k + 1)
                    pool.wait_ge(xh_ok, k + 1)
                    pool.tensor_tensor(a_l[:, k, :], xm[:, 0, :], a_h[:, k, :].bitcast(F32),
                                       ALU.subtract).then_inc(xl_ok, 1)

        tst = ExitStack()
        t_h = sb("t_hi", [128, 10, D], F32R, tst)
        t_l = sb("t_lo", [128, 10, D], F32R, tst)
        with stage() as st:
            za = sb("za", [128, TOK], F32, st)
            zb = sb("zb", [128, TOK], F32, st)
            awr = sb("ada_raw1", [128, 2, 1024], F32, st)
            pg = [st.enter_context(nc.psum_tensor(f"ps_in{g}", [128, 1536], F32)) for g in range(2)]
            pt = st.enter_context(nc.psum_tensor("ps_tr", [128, 512], F32))
            pa = st.enter_context(nc.psum_tensor("ps_ad", [128, 512], F32))
            z_ok, conv, cst, s_ok, fold, tr, th_ok, tl_ok, s_out, x0_out, a_in, pe_a, ad_ok = [
                sem(n, st) for n in ("z_ok", "conv", "cst", "s_ok", "fold", "tr", "th_ok", "tl_ok", "s_out", "x0_out",
                                 "a_in", "pe_a", "ad_ok")]
            a_in = [a_in, sem("a_in1", st)]
            block = st.enter_context(nc.Block())
            TR = ((0, 4, pt), (4, 8, pt), (8, 10, pa))

            @block.sync
            def _(sp):
                sp.sem_inc(x0_out, 1)

                def load_ada(m, i=None):
                    sp.dma_start(awr[:, m % 2, :], t["ada"][at(16 + m, i, 6), :, :]).then_inc(a_in[m % 2], 16)
                load_ada(0)
                load_ada(1)
                with sp.Fori(0, 4) as i:
                    for cc in range(2):
                        for role in range(3):
                            j = 3 * cc + role
                            load_entry(sp, e0 + 2 + j, wsrc(i * 6 + (e0 + 2 + j)), i, 6)
                            sp.wait_ge(pe_a, 1 + i * 6 + (j + 1))
                            load_ada(j + 2, i)
                            if role == 2:
                                sp.wait_ge(s_ok, i * 2 + (cc + 1))
                                sp.dma_start(s_d[i * 2 + cc, :, :], zb[:, :]).then_inc(s_out, 16)
                        sp.wait_ge(conv, 1 + i * 6 + (3 * cc + 3))
                        sp.dma_start(x0_d[i * 2 + cc, :, :], zb[:, :]).then_inc(x0_out, 16)
                for n in range(2):
                    sp.wait_ge(a_in[n], 16 * 13)
                sp.wait_ge(s_out, 128)
                sp.wait_ge(x0_out, 1 + 128)

            @block.gpsimd
            def _(pool):
                with pool.Fori(0, 4) as i:
                    for j in range(6):
                        split_lo(pool, e0 + 2 + j, i, 6)

            @block.scalar
            def _(act):
                def high(i, cc, r):
                    b0, b1, bank = TR[r]
                    act.wait_ge(tr, 1 + i * 6 + (3 * cc + r + 1))
                    act.activation(t_h[:, b0:b1, bass.ds(i * 256 + 128 * cc, 128)],
                                   bank[:, 0:128 * (b1 - b0)].rearrange("p (b c) -> p b c", c=128),
                                   ACT.Copy).then_inc(th_ok, 1)

                with act.Fori(0, 4) as i:
                    for cc in range(2):
                        for role in range(3):
                            j = 3 * cc + role
                            split_hi(act, e0 + 2 + j, i, 6)
                            if role == 2:
                                high(i, cc, 0)
                            act.wait_ge(w_used, i * 6 + (e0 + j + 1))
                            if role == 0:
                                act.wait_ge(tr, 1 + i * 6 + 3 * cc)
                                dst = za
                            elif role == 1:
                                act.wait_ge(x0_out, 1 + i * 32 + 16 * cc)
                                dst = zb
                            else:
                                act.wait_ge(s_out, i * 32 + (16 * cc + 16))
                                act.wait_ge(fold, i * 2 + (cc + 1))
                                dst = zb
                            tile = conv_p[:, bass.ds(i * 6 + j, 1), :]
                            act.activation(dst[:, :], pg[j % 2][:, 0:TOK], ACT.Identity,
                                           scale=tile[:, 0, 1:2], bias=tile[:, 0, 3:4]).then_inc(z_ok, 1)
                        high(i, cc, 1)
                        high(i, cc, 2)

            @block.vector
            def _(dve):
                dve.sem_inc(conv, 1)
                dve.sem_inc(tl_ok, 1)

                def low(i, cc, r):
                    b0, b1, bank = TR[r]
                    dve.wait_ge(th_ok, i * 6 + (3 * cc + r + 1))
                    cs = bass.ds(i * 256 + 128 * cc, 128)
                    dve.tensor_tensor(t_l[:, b0:b1, cs], bank[:, 0:128 * (b1 - b0)].rearrange("p (b c) -> p b c", c=128),
                                      t_h[:, b0:b1, cs].bitcast(F32), ALU.subtract).then_inc(tl_ok, 1)

                with dve.Fori(0, 4) as i:
                    for cc in range(2):
                        for role in range(3):
                            j = 3 * cc + role
                            if role == 2:
                                low(i, cc, 0)
                                dve.wait_ge(pe_a, 1 + i * 6 + (3 * cc + 3))
                                tiles = bass.ds(i * 6 + (16 + 3 * cc), 3)
                                dve.tensor_tensor(mod[:, tiles, :], pa[:, 0:6].rearrange("p (a b) -> p a b", b=2),
                                                  adab[:, tiles].unsqueeze(2).to_broadcast([128, 3, 2]),
                                                  ALU.add).then_inc(ad_ok, 1)
                            z, src = (za, zb, zb)[role], pg[j % 2]
                            w = conv_p[:, bass.ds(i * 6 + j, 1), :]
                            dve.wait_ge(z_ok, i * 6 + (j + 1))
                            for n, (p0, p1) in enumerate(PARTS):
                                ins = dve.scalar_tensor_tensor(z[:, p0 + 1:p1], src[:, p0:p1 - 1], w[:, 0, 0:1],
                                                               z[:, p0 + 1:p1], ALU.mult, ALU.add)
                            ins.then_inc(cst, 1)
                            dve.wait_ge(cst, i * 6 + (j + 1))
                            for n, (p0, p1) in enumerate(PARTS):
                                ins = dve.scalar_tensor_tensor(z[:, p0:p1 - 1], src[:, p0 + 1:p1], w[:, 0, 2:3],
                                                               z[:, p0:p1 - 1], ALU.mult, ALU.add)
                            ins.then_inc(conv, 1)
                            if role == 1:
                                dve.wait_ge(conv, 1 + i * 6 + (j + 1))
                                dve.tensor_tensor(zb[:, :], zb[:, :], za[:, :], ALU.mult).then_inc(s_ok, 1)
                                dve.wait_ge(s_ok, i * 2 + (cc + 1))
                                for p0, p1 in PARTS:
                                    h = (p1 - p0) // 2
                                    back = zb[:, p1 - 1:p0 + h - 1:-1]
                                    dve.tensor_tensor(za[:, p0:p0 + h], zb[:, p0:p0 + h], back, ALU.add)
                                    ins = dve.tensor_tensor(za[:, p0 + h:p1], zb[:, p0:p0 + h], back, ALU.subtract)
                                ins.then_inc(fold, 1)
                        low(i, cc, 1)
                        low(i, cc, 2)

            @block.tensor
            def _(pe):
                pe.sem_inc(tr, 1)
                pe.sem_inc(pe_a, 1)

                def transposes(r):
                    b0, b1, bank = TR[r]
                    for b in range(b0, b1):
                        last = pe.transpose(bank[:, (b - b0) * 128:(b - b0) * 128 + 128], za[:, b * 128:b * 128 + 128],
                                            ident[:, :])
                    last.then_inc(tr, 1)

                def ada_tile(i, cc, n):
                    m = 3 * cc + n
                    if n == 0:
                        pe.wait_ge(tl_ok, 1 + i * 6 + 3 * cc)
                    pe.wait_ge(a_in[m % 2], i * 48 + (16 * (m // 2) + 16))
                    for k in range(8):
                        last = pe.matmul(pa[:, 2 * n:2 * n + 2], awr[:, m % 2, k * 128:k * 128 + 128],
                                         silc[:, k, :], start=k == 0, stop=k == 7)
                    last.then_inc(pe_a, 1)

                with pe.Fori(0, 4) as i:
                    for cc in range(2):
                        for role in range(3):
                            j = 3 * cc + role
                            pe.wait_ge(w_split, i * 6 + (e0 + j + 1))
                            if j >= 2:
                                pe.wait_ge(conv, 1 + i * 6 + (j - 1))
                            elif role < 2:
                                pe.wait_ge(conv, 1 + i * 6)
                            for k in range(KT):
                                if role == 2 and k == 7:
                                    pe.wait_ge(fold, i * 2 + (cc + 1))
                                    pe.wait_ge(tl_ok, 1 + i * 6 + (3 * cc - 1))
                                    transposes(0)
                                last = products(pe, e0 + j, [(k, a_h[:, k, :], a_l[:, k, :], pg[j % 2])], CHUNKS,
                                                k == 0, k == KT - 1)
                                if k == KT - 1:
                                    last.then_inc(w_used, 1)
                                if k == 3:
                                    ada_tile(i, cc, role)
                        pe.wait_ge(tl_ok, 1 + i * 6 + (3 * cc + 1))
                        transposes(1)
                        pe.wait_ge(ad_ok, i * 2 + (cc + 1))
                        transposes(2)
        e0 += E_IN

        with stage() as st:
            gsl = sb("g_spec", [128, 2, 2, 512], F32, st)
            yb = sb("y_spec", [128, 2, 2, 512], F32, st)
            pr = sb("y_prod", [128, 2, 512], F32, st)
            pf = [st.enter_context(nc.psum_tensor(f"ps_fw{g}", [128, 2048], F32)) for g in range(2)]
            g_in, y_out = [sem("g_in0", st), sem("g_in1", st)], [sem("y_out0", st), sem("y_out1", st)]
            pr_ok, y_ok = sem("pr_ok", st), sem("y_ok", st)
            block = st.enter_context(nc.Block())

            def rounds(step, eng):
                with eng.Fori(0, 3) as i:
                    step(0, i)
                    step(1, i)
                for f in range(6, 10):
                    step(f, None)

            @block.sync
            def _(sp):
                sp.sem_inc(y_out[0], 1)
                sp.sem_inc(y_out[1], 1)

                def step(f, i):
                    if f < 7:
                        load_entry(sp, e0 + 2 + f, wsrc(at(e0 + 2 + f, i, 2)), i, 2)
                    for hf in range(2):
                        sp.wait_ge(y_ok, at(1 + 2 * f + hf + 1, i, 4))
                        for pm in range(2):
                            if f < 8:
                                dst = y_d[4 * hf:4 * hf + 4, (pm + f) % 2, :, at(f, i, 2), :]
                            else:
                                dst = y_d[4 * hf:4 * hf + 4, 2, :, 2 * (f - 8) + pm, :]
                            sp.dma_start(dst.rearrange("c p n -> p c n"),
                                         yb[:, hf, pm, :].rearrange("p (c n) -> p c n", n=128)).then_inc(y_out[hf], 16)
                rounds(step, sp)
                for hf in range(2):
                    sp.wait_ge(y_out[hf], 321)

            @block.scalar
            def _(act):
                def step(f, i):
                    for hf in range(2):
                        act.wait_ge(pr_ok, at(2 * f + hf + 2, i, 4))
                        act.dma_start(gsl[:, hf, :, :], spec[at(f, i, 2), :, :, hf * 512:hf * 512 + 512]).then_inc(
                            g_in[hf], 16)
                    if f < 7:
                        split_hi(act, e0 + 2 + f, i, 2)
                rounds(step, act)

            @block.gpsimd
            def _(pool):
                pool.sem_inc(y_ok, 1)

                def step(f, i):
                    for hf in range(2):
                        pool.wait_ge(pr_ok, at(2 * f + hf + 4, i, 4))
                        pool.tensor_tensor(yb[:, hf, 0, :], yb[:, hf, 0, :], pr[:, 0, :], ALU.add)
                        pool.tensor_tensor(yb[:, hf, 1, :], yb[:, hf, 1, :], pr[:, 1, :],
                                           ALU.subtract).then_inc(y_ok, 1)
                    if f < 7:
                        split_lo(pool, e0 + 2 + f, i, 2)
                rounds(step, pool)

            @block.vector
            def _(dve):
                dve.sem_inc(pr_ok, 3)

                def step(f, i):
                    dve.wait_ge(w_used, at(e0 + min(f, 8) + 1, i, 2))
                    for hf in range(2):
                        c0, c1 = hf * 512, hf * 512 + 512
                        p, m = pf[f % 2][:, c0:c1], pf[f % 2][:, 1024 + c0:1024 + c1]
                        dve.wait_ge(g_in[hf], at(16 * f + 16, i, 32))
                        dve.wait_ge(y_out[hf], at(1 + 32 * f, i, 64))
                        dve.wait_ge(y_ok, at(1 + 2 * f + hf, i, 4))
                        dve.tensor_tensor(yb[:, hf, 0, :], p, gsl[:, hf, 0, :], ALU.mult)
                        dve.tensor_tensor(pr[:, 0, :], m, gsl[:, hf, 1, :], ALU.mult)
                        dve.tensor_tensor(yb[:, hf, 1, :], m, gsl[:, hf, 0, :], ALU.mult)
                        dve.tensor_tensor(pr[:, 1, :], p, gsl[:, hf, 1, :], ALU.mult).then_inc(pr_ok, 1)
                rounds(step, dve)

            @block.tensor
            def _(pe):
                def step(f, i):
                    if f == 9:
                        return
                    pe.wait_ge(w_split, at(e0 + f + 1, i, 2))
                    pe.wait_ge(pr_ok, at(2 * f + 1, i, 4) if f < 8 else 2 * f + 3)
                    if f < 8:
                        for pm in range(2):
                            base = 4 * ((pm + f) % 2)
                            last = products(pe, e0 + f, [
                                (4 * pm + k, t_h[:, base + k, :], t_l[:, base + k, :],
                                 pf[f % 2][:, pm * 1024:pm * 1024 + 1024]) for k in range(4)], ((0, 512), (512, 1024)))
                    else:
                        for ab in range(2):
                            for pm in range(2):
                                last = products(pe, e0 + 8, [
                                    (4 * ab + 2 * pm + k, t_h[:, 8 + k, :], t_l[:, 8 + k, :],
                                     pf[ab][:, pm * 1024:pm * 1024 + 1024]) for k in range(2)], ((0, 512), (512, 1024)))
                    last.then_inc(w_used, 1)
                rounds(step, pe)
        tst.close()
        e0 += E_FWD

        w0 = e0
        with stage() as st:
            ib_h = sb("ib_hi", [128, 18, 512], F32R, st)
            ib_l = sb("ib_lo", [128, 18, 512], F32R, st)
            sx = sb("sx", [128, 2, 2 * TOK], F32, st)
            yt = sb("yt", [128, TOK], F32, st)
            an = sb("anti", [128, 512], F32, st)
            pi = [st.enter_context(nc.psum_tensor(f"ps_iv{g}", [128, 1536], F32)) for g in range(2)]
            b_in, bh_ok, bl_ok, sx_in, an_ok, yp_ok, ya, yb2, g_ok, ah_ok, al_ok = [
                sem(n, st) for n in ("b_in", "bh_ok", "bl_ok", "sx_in", "an_ok", "yp_ok", "ya", "yb", "g_ok", "ah_ok", "al_ok")]
            b_in, sx_in = [b_in, sem("b_in1", st)], [sx_in, sem("sx_in1", st)]
            block = st.enter_context(nc.Block())

            def rounds(step, eng):
                with eng.Fori(0, 3) as i:
                    step(0, i)
                    step(1, i)
                step(6, None)
                step(7, None)

            @block.sync
            def _(sp):
                for j in range(2):
                    load_entry(sp, e0 + j, y_d[0, j, :, :, :].rearrange("p f n -> p (f n)"))
                for n in range(5):
                    if n >= 2:
                        sp.wait_ge(bl_ok, n - 1)
                    src = t["inv"][n, :, :] if n < 4 else t["inv_p"]
                    sp.dma_start(sx[:, n % 2, 0:src.shape[1]], src).then_inc(b_in[n % 2], 16)
                sp.wait_ge(bl_ok, 5)

                def step(c, i):
                    sp.wait_ge(al_ok, at(c + 1, i, 2))
                    sp.dma_start(sx[:, c % 2, 0:TOK], s_d[at(c, i, 2), :, :]).then_inc(sx_in[c % 2], 16)
                    sp.dma_start(sx[:, c % 2, TOK:2 * TOK], x0_d[at(c, i, 2), :, :]).then_inc(sx_in[c % 2], 16)
                    for j in range(3):
                        n = 3 * c + j + 2
                        if n < E_INV:
                            src = y_d[at(n // 3, i, 2), n % 3, :, :, :].rearrange("p f n -> p (f n)")
                            width = 512 if n % 3 == 2 else 1024
                            load_entry(sp, e0 + n, src[:, 0:width], i, 6, width)
                        else:
                            load_entry(sp, e0 + n, wsrc(w0 + n - E_INV), i, 6)
                rounds(step, sp)

            @block.gpsimd
            def _(pool):
                split_lo(pool, e0)
                split_lo(pool, e0 + 1)

                def step(c, i):
                    for j in range(3):
                        n = 3 * c + j + 2
                        split_lo(pool, e0 + n, i, 6, 512 if n < E_INV and n % 3 == 2 else 1024)
                rounds(step, pool)

            @block.scalar
            def _(act):
                split_hi(act, e0)
                split_hi(act, e0 + 1)
                for n in range(5):
                    w = 4 if n < 4 else 2
                    act.wait_ge(b_in[n % 2], 16 * (n // 2) + 16)
                    act.activation(ib_h[:, 4 * n:4 * n + w, :],
                                   sx[:, n % 2, 0:512 * w].rearrange("p (a b) -> p a b", b=512),
                                   ACT.Copy).then_inc(bh_ok, 1)

                def step(c, i):
                    for j in range(3):
                        n = 3 * c + j + 2
                        split_hi(act, e0 + n, i, 6, 512 if n < E_INV and n % 3 == 2 else 1024)
                        act.wait_ge(w_used, at(e0 + 3 * c + j + 1, i, 6))
                        if j == 1:
                            act.wait_ge(al_ok, at(c + 2, i, 2))
                            act.activation(an[:, :], pi[c % 2][:, 512:1024], ACT.Copy).then_inc(an_ok, 1)
                        if j == 2:
                            act.activation(yt[:, LS:TOK], pi[c % 2][:, 1024:1280], ACT.Copy).then_inc(yp_ok, 1)
                    act.wait_ge(g_ok, at(c + 1, i, 2))
                    act.activation(a_h[:, bass.ds(at(c, i, 2), 1), :], yt[:, :].unsqueeze(1), ACT.Copy).then_inc(ah_ok, 1)
                rounds(step, act)

            @block.vector
            def _(dve):
                dve.sem_inc(al_ok, 2)
                for n in range(5):
                    w = 4 if n < 4 else 2
                    dve.wait_ge(bh_ok, n + 1)
                    dve.tensor_tensor(ib_l[:, 4 * n:4 * n + w, :],
                                      sx[:, n % 2, 0:512 * w].rearrange("p (a b) -> p a b", b=512),
                                      ib_h[:, 4 * n:4 * n + w, :].bitcast(F32), ALU.subtract).then_inc(bl_ok, 1)

                def step(c, i):
                    sym = pi[c % 2][:, 0:512]
                    dve.wait_ge(an_ok, at(c + 1, i, 2))
                    dve.tensor_tensor(yt[:, 0:512], sym, an[:, :], ALU.add)
                    dve.tensor_tensor(yt[:, 1023:511:-1], sym, an[:, :], ALU.subtract).then_inc(ya, 1)
                    dve.wait_ge(ya, at(c + 1, i, 2))
                    dve.wait_ge(yp_ok, at(c + 1, i, 2))
                    dve.wait_ge(sx_in[c % 2], at(32 * (c // 2) + 32, i, 32))
                    dve.scalar_tensor_tensor(yt[:, :], sx[:, c % 2, 0:TOK], hb_p[:, bass.ds(at(c, i, 2), 1)],
                                             yt[:, :], ALU.mult, ALU.add).then_inc(yb2, 1)
                    dve.wait_ge(yb2, at(c + 1, i, 2))
                    dve.tensor_tensor(yt[:, :], yt[:, :], sx[:, c % 2, TOK:2 * TOK], ALU.mult).then_inc(g_ok, 1)
                    dve.wait_ge(g_ok, at(c + 1, i, 2))
                    dve.wait_ge(ah_ok, at(c + 1, i, 2))
                    dve.tensor_tensor(a_l[:, bass.ds(at(c, i, 2), 1), :], yt[:, :].unsqueeze(1),
                                      a_h[:, bass.ds(at(c, i, 2), 1), :].bitcast(F32), ALU.subtract).then_inc(al_ok, 1)
                rounds(step, dve)

            @block.tensor
            def _(pe):
                pe.wait_ge(bl_ok, 5)

                def step(c, i):
                    out = pi[c % 2]
                    for j in range(3):
                        pe.wait_ge(w_split, at(e0 + 3 * c + j + 1, i, 6))
                        if j == 0:
                            pe.wait_ge(al_ok, at(c + 1, i, 2))
                        if j < 2:
                            use = [2 * f + (f + j) % 2 for f in range(8)]
                            last = products(pe, e0 + 3 * c + j, [
                                (f, ib_h[:, u, :], ib_l[:, u, :], out[:, 512 * j:512 * j + 512])
                                for f, u in enumerate(use)], ((0, 512),))
                        else:
                            bh = ib_h[:, 16:18, :].rearrange("p a (b n) -> p (a b) n", n=256)
                            bl = ib_l[:, 16:18, :].rearrange("p a (b n) -> p (a b) n", n=256)
                            last = products(pe, e0 + 3 * c + 2, [
                                (b, bh[:, b, :], bl[:, b, :], out[:, 1024:1280]) for b in range(4)], ((0, 256),))
                        last.then_inc(w_used, 1)
                rounds(step, pe)
        e0 += E_INV
        wsh = E_INV

        def stage_out(layer, e0, xt, s1, s2):
            with stage() as st:
                sq = sb("sq", [128, 2, TOK], F32, st)
                pg = [st.enter_context(nc.psum_tensor(f"ps_out{layer}{g}", [128, 1536], F32)) for g in range(2)]
                x_in, xs_ok, x_ok, sq_ok, s1_ok, s2_ok = [
                    sem(n, st) for n in ("x_in", "xs_ok", "x_ok", "sq_ok", "s1_ok", "s2_ok")]
                block = st.enter_context(nc.Block())

                @block.sync
                def _(sp):
                    src = t["x"] if layer == 0 else x_d
                    for k in range(KT):
                        sp.dma_start(xt[:, k, :], src[k, :, :]).then_inc(x_in, 16)
                    with sp.Fori(0, 4) as i:
                        for j in range(2):
                            load_entry(sp, e0 + 2 + j, wsrc(i * 2 + (e0 + 2 + j - wsh)), i, 2)

                @block.gpsimd
                def _(pool):
                    pool.memset(s1[:, :], 0.0).then_inc(s1_ok, 1)
                    with pool.Fori(0, 4) as i:
                        for j in range(2):
                            pool.wait_ge(x_ok, i * 2 + (j + 3))
                            pool.wait_ge(s1_ok, i * 2 + (j + 1))
                            pool.tensor_tensor(s1[:, :], s1[:, :], xt[:, i * 2 + j, :], ALU.add).then_inc(s1_ok, 1)
                            split_lo(pool, e0 + 2 + j, i, 2)

                @block.scalar
                def _(act):
                    act.wait_ge(x_in, 128)
                    if layer == 0:
                        act.activation(xt[:, :, :], xt[:, :, :], ACT.Copy, scale=ALPHA).then_inc(xs_ok, 1)
                    else:
                        act.sem_inc(xs_ok, 1)
                    with act.Fori(0, 4) as i:
                        for j in range(2):
                            split_hi(act, e0 + 2 + j, i, 2)
                            act.wait_ge(x_ok, i * 2 + (j + 3))
                            act.wait_ge(s2_ok, i * 2 + (j + 1))
                            act.activation(sq[:, j, :], xt[:, i * 2 + j, :], ACT.Square).then_inc(sq_ok, 1)

                @block.vector
                def _(dve):
                    dve.sem_inc(x_ok, 2)
                    dve.memset(s2[:, :], 0.0).then_inc(s2_ok, 2)
                    dve.wait_ge(xs_ok, 1)
                    with dve.Fori(0, 4) as i:
                        for j in range(2):
                            dve.wait_ge(w_used, i * 2 + (e0 + j + 1))
                            gate = mod[:, bass.ds(i * 2 + (layer * 48 + G1 * 8 + j), 1), :]
                            for p, (p0, p1) in enumerate(PARTS):
                                ins = dve.scalar_tensor_tensor(xt[:, i * 2 + j, p0:p1], pg[j][:, p0:p1],
                                                               gate[:, 0, p:p + 1], xt[:, i * 2 + j, p0:p1],
                                                               ALU.mult, ALU.add)
                            ins.then_inc(x_ok, 1)
                            dve.wait_ge(sq_ok, i * 2 + (j + 1))
                            dve.wait_ge(s2_ok, i * 2 + (j + 2))
                            dve.tensor_tensor(s2[:, :], s2[:, :], sq[:, j, :], ALU.add).then_inc(s2_ok, 1)

                @block.tensor
                def _(pe):
                    with pe.Fori(0, 4) as i:
                        for j in range(2):
                            pe.wait_ge(w_split, i * 2 + (e0 + j + 1))
                            pe.wait_ge(x_ok, i * 2 + (j + 1))
                            products(pe, e0 + j, [(k, a_h[:, k, :], a_l[:, k, :], pg[j]) for k in range(KT)],
                                     CHUNKS).then_inc(w_used, 1)

        def stage_norm(layer, ln, xt, s1, s2, then):
            with stage() as st:
                mu = sb("mu", [128, TOK], F32, st)
                rstd = sb("rstd", [128, TOK], F32, st)
                xn = sb("xn", [128, 2, TOK], F32, st)
                xm = sb("xm2", [128, 2, TOK], F32, st)
                pm = st.enter_context(nc.psum_tensor(f"ps_mean{layer}{ln}", [128, 1536], F32))
                pv = st.enter_context(nc.psum_tensor(f"ps_sq{layer}{ln}", [128, 1536], F32))
                stat, mu_ok, v_ok, sd_ok, rs_ok, coef, xc_ok, xn_ok, xm_ok, xh_ok, xl_ok, xa_ok, x_out = [
                    sem(n, st) for n in ("stat", "mu_ok", "v_ok", "sd_ok", "rs_ok", "coef", "xc_ok", "xn_ok", "xm_ok", "xh_ok",
                                     "xl_ok", "xa_ok", "x_out")]
                g0, g1 = {0: (0, 6), 2: (6, 12), 4: (12, 14), 6: (0, 0)}[ln]
                groups = g1 - g0
                if groups:
                    awr = sb("ada_raw2", [128, 2, 4, 512], F32, st)
                    row = sb("ada_row", [2, 512], F32, st)
                    pa = st.enter_context(nc.psum_tensor(f"ps_ar{ln}", [128, 512], F32))
                    pt = st.enter_context(nc.psum_tensor(f"ps_at{ln}", [128, 512], F32))
                    a_in, pe_a = [sem("a_in0", st), sem("a_in1", st)], sem("pe_a", st)
                    row_ok, row_t = sem("row_ok", st), sem("row_t", st)
                block = st.enter_context(nc.Block())

                @block.sync
                def _(sp):
                    for n in range(2 * groups):
                        if n >= 2:
                            sp.wait_ge(pe_a, n - 1)
                        src = t["ada_g"][g0 + n // 2, :, 2048 * (n % 2):2048 * (n % 2) + 2048]
                        sp.dma_start(awr[:, n % 2, :, :].rearrange("p a b -> p (a b)"), src).then_inc(a_in[n % 2], 16)
                    if then != "ffn":
                        for k in range(KT):
                            sp.wait_ge(xa_ok, k + 1)
                            sp.dma_start((x_d if then == "qkv" else t["y"])[k, :, :], xt[:, k, :]).then_inc(x_out, 16)
                    if then != "ffn":
                        sp.wait_ge(x_out, 128)

                @block.tensor
                def _(pe):
                    for ps, src in ((pm, s1), (pv, s2)):
                        for c0, c1 in CHUNKS:
                            last = pe.matmul(ps[:, c0:c1], meanw[:, :], src[:, c0:c1], start=True, stop=True)
                        last.then_inc(stat, 1)
                    def transposes(g):
                        pe.wait_ge(row_ok, g + 1)
                        for q in range(4):
                            c = 8 * g + 2 * q
                            last = pe.transpose(pt[:, c:c + 2], row[:, 128 * q:128 * q + 128], ident[0:2, 0:2])
                        last.then_inc(row_t, 1)

                    for g in range(groups):
                        if g:
                            pe.wait_ge(row_ok, g)
                        for half in range(2):
                            pe.wait_ge(a_in[half], 16 * g + 16)
                            for k in range(4):
                                last = pe.matmul(pa[0:2, :], silc[:, 4 * half + k, :], awr[:, half, k, :],
                                                 start=half == 0 and k == 0, stop=half == 1 and k == 3)
                            last.then_inc(pe_a, 1)
                        if g:
                            transposes(g - 1)
                    if groups:
                        transposes(groups - 1)

                @block.scalar
                def _(act):
                    act.wait_ge(stat, 1)
                    act.activation(mu[:, :], pm[:, 0:TOK], ACT.Copy).then_inc(mu_ok, 1)
                    act.wait_ge(v_ok, 3)
                    act.activation(rstd[:, :], rstd[:, :], ACT.Sqrt, bias=eps[:, :]).then_inc(sd_ok, 1)

                    def to_row(g):
                        if g < groups:
                            act.wait_ge(pe_a, 2 * g + 2)
                            if g:
                                act.wait_ge(row_t, g)
                            act.activation(row[:, :], pa[0:2, :], ACT.Copy).then_inc(row_ok, 1)
                    to_row(0)
                    to_row(1)
                    for k in range(KT):
                        if k in (2, 3, 5):
                            to_row(k if k < 4 else 4)
                        act.wait_ge(xn_ok, k + 1)
                        if then != "end":
                            for p, (p0, p1) in enumerate(PARTS):
                                ins = act.activation(a_h[:, k, p0:p1], xn[:, k % 2, p0:p1], ACT.Identity,
                                                     scale=aff[:, 0, k, p:p + 1], bias=aff[:, 1, k, p:p + 1])
                            ins.then_inc(xh_ok, 1)
                            g, b = axs[:, 0, k:k + 1], axs[:, 1, k:k + 1]
                        else:
                            g, b = ln_p[:, ln, k:k + 1], ln_p[:, ln + 1, k:k + 1]
                        act.activation(xt[:, k, :], xn[:, k % 2, :], ACT.Identity, scale=g, bias=b).then_inc(xa_ok, 1)
                    to_row(5)

                @block.vector
                def _(dve):
                    if then == "ffn":
                        modulation(dve, coef, layer, SC2, SH2, ln)
                    elif then == "qkv":
                        modulation(dve, coef, 1, SC1, SH1, ln)
                    dve.wait_ge(mu_ok, 1)
                    dve.tensor_tensor(rstd[:, :], mu[:, :], mu[:, :], ALU.mult).then_inc(v_ok, 1)
                    dve.wait_ge(v_ok, 1)
                    dve.wait_ge(stat, 2)
                    dve.tensor_tensor(rstd[:, :], pv[:, 0:TOK], rstd[:, :], ALU.subtract).then_inc(v_ok, 1)
                    dve.wait_ge(v_ok, 2)
                    dve.tensor_scalar(rstd[:, :], rstd[:, :], 0.0, None, ALU.max).then_inc(v_ok, 1)
                    dve.wait_ge(sd_ok, 1)
                    dve.reciprocal(rstd[:, :], rstd[:, :]).then_inc(rs_ok, 1)
                    dve.wait_ge(rs_ok, 1)
                    for k in range(KT + 1):
                        if k < KT:
                            if k >= 2:
                                dve.wait_ge(xa_ok, k - 1)
                            dve.tensor_tensor(xn[:, k % 2, :], xt[:, k, :], mu[:, :], ALU.subtract).then_inc(xc_ok, 1)
                            dve.wait_ge(xc_ok, k + 1)
                            dve.tensor_tensor(xn[:, k % 2, :], xn[:, k % 2, :], rstd[:, :], ALU.mult).then_inc(xn_ok, 1)
                        if k >= 1 and then != "end":
                            if k >= 3:
                                dve.wait_ge(xl_ok, k - 2)
                            dve.wait_ge(xn_ok, k)
                            for p, (p0, p1) in enumerate(PARTS):
                                ins = dve.tensor_scalar(xm[:, (k - 1) % 2, p0:p1], xn[:, (k - 1) % 2, p0:p1],
                                                        aff[:, 0, k - 1, p:p + 1], aff[:, 1, k - 1, p:p + 1],
                                                        ALU.mult, ALU.add)
                            ins.then_inc(xm_ok, 1)
                            dve.wait_ge(xm_ok, k)
                    if groups:
                        dve.wait_ge(row_t, groups)
                        m0, m1 = 40 + 4 * g0, 40 + 4 * g1
                        dve.tensor_tensor(mod[:, m0:m1, :], pt[:, 0:2 * (m1 - m0)].rearrange("p (a b) -> p a b", b=2),
                                          adab[:, m0:m1].unsqueeze(2).to_broadcast([128, m1 - m0, 2]), ALU.add)

                @block.gpsimd
                def _(pool):
                    if then != "end":
                        for k in range(KT):
                            pool.wait_ge(xm_ok, k + 1)
                            pool.wait_ge(xh_ok, k + 1)
                            pool.tensor_tensor(a_l[:, k, :], xm[:, k % 2, :], a_h[:, k, :].bitcast(F32),
                                               ALU.subtract).then_inc(xl_ok, 1)

        def stage_ffn(layer, e0, xt, s1, s2, last_stage):
            with stage() as st:
                hh = sb("hid_hi", [128, 2, 2, TOK], F32R, st)
                hl = sb("hid_lo", [128, 2, 2, TOK], F32R, st)
                sg = sb("silu_g", [128, TOK], F32, st)
                hf = sb("hid", [128, TOK], F32, st)
                pg = [st.enter_context(nc.psum_tensor(f"ps_ff{layer}{g}", [128, 1536], F32)) for g in range(2)]
                silu, gated, hh_ok, hl_ok, out_mm, out_ok, sq_ok, s1_ok, s2_ok = [
                    sem(n, st) for n in ("silu", "gated", "hh_ok", "hl_ok", "out_mm", "out_ok", "sq_ok", "s1_ok", "s2_ok")]
                block = st.enter_context(nc.Block())

                def rounds(step_in, step_out, eng):
                    step_in(0, e0, None)
                    with eng.Fori(0, 5) as r:
                        for q in range(2):
                            step_in(1 + q, e0 + 4 + 6 * q, r)
                            step_out(q, e0 + 8 + 6 * q, r)
                    step_out(FC - 1, e0 + E_FFN - 2, None)

                @block.sync
                def _(sp):
                    def load(n, e, r):
                        for j in range(n):
                            if last_stage and r is None and e + 2 + j >= e0 + E_FFN:
                                continue
                            load_entry(sp, e + 2 + j, wsrc(at(e + 2 + j - wsh, r, 12)), r, 12)
                    rounds(lambda i, e, r: load(4, e, r), lambda i, e, r: load(2, e, r), sp)

                @block.scalar
                def _(act):
                    def step_in(i, e, r):
                        for k in range(2):
                            act.wait_ge(w_used, at(e + 2 * k + 1, r, 12))
                            if not (r is None and k == 0):
                                act.wait_ge(gated, at(2 * i + k, r, 4))
                            act.activation(sg[:, :], pg[0][:, 0:TOK], ACT.Silu).then_inc(silu, 1)
                            split_hi(act, e + 2 + 2 * k, r, 12)
                            act.wait_ge(gated, at(2 * i + k + 1, r, 4))
                            act.activation(hh[:, i % 2, k, :], hf[:, :], ACT.Copy).then_inc(hh_ok, 1)
                            split_hi(act, e + 3 + 2 * k, r, 12)

                    def step_out(i, e, r):
                        if r is not None:
                            for j in range(2):
                                split_hi(act, e + 2 + j, r, 12)
                        else:
                            for m in range(8):
                                act.wait_ge(out_ok, 8 + 8 * i + m + 1)
                                if m >= 2:
                                    act.wait_ge(s2_ok, m)
                                act.activation((sg, hf)[m % 2][:, :], xt[:, m, :], ACT.Square).then_inc(sq_ok, 1)
                                if m % 4 == 3 and not last_stage:
                                    split_hi(act, e + 2 + m // 4)
                    rounds(step_in, step_out, act)

                @block.gpsimd
                def _(pool):
                    pool.memset(s1[:, :], 0.0).then_inc(s1_ok, 1)

                    def step_in(i, e, r):
                        for k in range(2):
                            split_lo(pool, e + 2 + 2 * k, r, 12)
                            pool.wait_ge(hh_ok, at(2 * i + k + 1, r, 4))
                            pool.tensor_tensor(hl[:, i % 2, k, :], hf[:, :], hh[:, i % 2, k, :].bitcast(F32),
                                               ALU.subtract).then_inc(hl_ok, 1)
                            split_lo(pool, e + 3 + 2 * k, r, 12)

                    def step_out(i, e, r):
                        if r is not None:
                            for j in range(2):
                                split_lo(pool, e + 2 + j, r, 12)
                        else:
                            for m in range(8):
                                pool.wait_ge(out_ok, 8 + 8 * i + m + 1)
                                pool.wait_ge(s1_ok, m + 1)
                                pool.tensor_tensor(s1[:, :], s1[:, :], xt[:, m, :], ALU.add).then_inc(s1_ok, 1)
                                if m % 4 == 3 and not last_stage:
                                    split_lo(pool, e + 2 + m // 4)
                    rounds(step_in, step_out, pool)

                @block.vector
                def _(dve):
                    dve.sem_inc(out_ok, 8)
                    dve.memset(s2[:, :], 0.0).then_inc(s2_ok, 1)

                    def step_in(i, e, r):
                        for k in range(2):
                            dve.wait_ge(w_used, at(e + 2 * k + 2, r, 12))
                            dve.wait_ge(silu, at(2 * i + k + 1, r, 4))
                            if not (r is None and k == 0):
                                dve.wait_ge(hl_ok, at(2 * i + k, r, 4))
                            dve.tensor_tensor(hf[:, :], sg[:, :], pg[1][:, 0:TOK], ALU.mult).then_inc(gated, 1)

                    def step_out(i, e, r):
                        for m in range(8):
                            if m % 4 == 3:
                                dve.wait_ge(w_used, at(e + m // 4 + 1, r, 12))
                            else:
                                dve.wait_ge(out_mm, at(6 * i + 3 * (m // 4) + m % 4 + 1, r, 12))
                            gate = mod[:, layer * 48 + G2 * 8 + m, :]
                            if i or r is not None:
                                dve.wait_ge(out_ok, at(8 + 8 * i + m - 7, r, 16))
                            for p, (p0, p1) in enumerate(PARTS):
                                ins = dve.scalar_tensor_tensor(xt[:, m, p0:p1], pg[m % 2][:, p0:p1], gate[:, p:p + 1],
                                                               xt[:, m, p0:p1], ALU.mult, ALU.add)
                            ins.then_inc(out_ok, 1)
                            if r is None and m >= 1:
                                dve.wait_ge(sq_ok, m)
                                dve.wait_ge(s2_ok, m)
                                dve.tensor_tensor(s2[:, :], s2[:, :], (sg, hf)[(m - 1) % 2][:, :],
                                                  ALU.add).then_inc(s2_ok, 1)
                        if r is None:
                            dve.wait_ge(sq_ok, 8)
                            dve.wait_ge(s2_ok, 8)
                            dve.tensor_tensor(s2[:, :], s2[:, :], hf[:, :], ALU.add).then_inc(s2_ok, 1)
                    rounds(step_in, step_out, dve)
                @block.tensor
                def _(pe):
                    def step_in(i, e, r):
                        for j in range(4):
                            pe.wait_ge(w_split, at(e + j + 1, r, 12))
                            if j < 2 and r is not None:
                                pe.wait_ge((silu, gated)[j], at(2 * i, r, 4))
                                pe.wait_ge(out_ok, at(8 * (i - 1) + 7 + j, r, 16))
                            elif j >= 2:
                                pe.wait_ge((silu, gated)[j % 2], at(2 * i + 1, r, 4))
                            products(pe, e + j, [(k, a_h[:, k, :], a_l[:, k, :], pg[j % 2]) for k in range(KT)],
                                     CHUNKS).then_inc(w_used, 1)

                    def step_out(i, e, r):
                        pe.wait_ge(hl_ok, at(2 * i + 2, r, 4))
                        for m in range(8):
                            if m % 4 == 0:
                                pe.wait_ge(w_split, at(e + m // 4 + 1, r, 12))
                            if m < 2 and r is not None:
                                pe.wait_ge((silu, gated)[m], at(2 * i + 4, r, 4))
                            elif m < 2:
                                pe.wait_ge(out_ok, 8 * i + 7 + m)
                            else:
                                pe.wait_ge(out_ok, at(8 + 8 * i + m - 1, r, 16))
                            last = products(pe, e + m // 4, [(2 * (m % 4) + k, hh[:, i % 2, k, :], hl[:, i % 2, k, :],
                                                              pg[m % 2]) for k in range(2)], CHUNKS)
                            last.then_inc(w_used if m % 4 == 3 else out_mm, 1)
                    rounds(step_in, step_out, pe)

        def stage_qkv(e0):
            with stage() as st:
                z = sb("z_qkv", [128, 2, TOK], F32, st)
                pg = [st.enter_context(nc.psum_tensor(f"ps_qkv{g}", [128, 1536], F32)) for g in range(2)]
                z_ok, z_out = [sem("z_ok0", st), sem("z_ok1", st)], [sem("z_out0", st), sem("z_out1", st)]
                block = st.enter_context(nc.Block())

                @block.sync
                def _(sp):
                    for j in range(2):
                        sp.sem_inc(z_out[j], 1)
                    with sp.Fori(0, 12) as i:
                        for j in range(2):
                            load_entry(sp, e0 + 2 + j, wsrc(i * 2 + (e0 + 2 + j - wsh)), i, 2)
                            sp.wait_ge(z_ok[j], i + 2)
                            sp.dma_start(qkv_d[i * 2 + j, :, :], z[:, j, :]).then_inc(z_out[j], 16)
                    for j in range(2):
                        sp.wait_ge(z_out[j], 1 + 16 * 12)

                @block.gpsimd
                def _(pool):
                    with pool.Fori(0, 12) as i:
                        for j in range(2):
                            split_lo(pool, e0 + 2 + j, i, 2)

                @block.scalar
                def _(act):
                    act.sem_inc(z_ok[0], 1)
                    with act.Fori(0, 12) as i:
                        for j in range(2):
                            split_hi(act, e0 + 2 + j, i, 2)
                            if j == 0:
                                act.wait_ge(w_used, i * 2 + (e0 + 1))
                                act.wait_ge(z_out[0], i * 16 + 1)
                                act.activation(z[:, 0, :], pg[0][:, 0:TOK], ACT.Copy).then_inc(z_ok[0], 1)

                @block.vector
                def _(dve):
                    dve.sem_inc(z_ok[1], 1)
                    with dve.Fori(0, 12) as i:
                        dve.wait_ge(w_used, i * 2 + (e0 + 2))
                        dve.wait_ge(z_out[1], i * 16 + 1)
                        dve.tensor_copy(z[:, 1, :], pg[1][:, 0:TOK]).then_inc(z_ok[1], 1)

                @block.tensor
                def _(pe):
                    with pe.Fori(0, 12) as i:
                        for j in range(2):
                            pe.wait_ge(w_split, i * 2 + (e0 + j + 1))
                            pe.wait_ge(z_ok[j], i + 1)
                            products(pe, e0 + j, [(k, a_h[:, k, :], a_l[:, k, :], pg[j]) for k in range(KT)],
                                     CHUNKS).then_inc(w_used, 1)

        def layer_rest(layer, e0):
            with ExitStack() as st:
                xt = sb("x_t", [128, KT, TOK], F32, st)
                s1 = sb("sum_x", [128, TOK], F32, st)
                s2 = sb("sum_xx", [128, TOK], F32, st)
                stage_out(layer, e0, xt, s1, s2)
                stage_norm(layer, 4 * layer, xt, s1, s2, "ffn")
                stage_ffn(layer, e0 + E_OUT, xt, s1, s2, layer == 1)
                stage_norm(layer, 4 * layer + 2, xt, s1, s2, "end" if layer else "qkv")
            return e0 + E_OUT + E_FFN

        e0 = layer_rest(0, e0)
        stage_qkv(e0)
        e0 += E_QKV

        with stage() as st:
            U = 20
            qr = sb("q_raw", [128, TOK], F32, st)
            kr = sb("k_raw", [128, 2304], F32, st)
            qh = sb("q_hl", [128, 2, TOK], F32R, st)
            kh = sb("k_hi", [128, 2, 1536], F32R, st)
            kl = sb("k_lo", [128, 2, 1536], F32R, st)
            vh = sb("v_hi", [128, 20, 128], F32R, st)
            vl = sb("v_lo", [128, 20, 128], F32R, st)
            bias = sb("rpb_t", [128, 2, 16, RPB_W], F32, st)
            pb = sb("probs", [128, 3, 640], F32, st)
            vc = sb("v_cache", [128, 2, 128], F32, st)
            pth = sb("pt_hi", [128, 2, 5, 128], F32R, st)
            ptl = sb("pt_lo", [128, 2, 5, 128], F32R, st)
            mask = sb("mask", [128, 6, 384], BF16, st)
            ident_b = sb("ident_b", [128, 128], BF16, st)
            stat = sb("stat", [128, 4, 8], F32, st)
            ps_s = [st.enter_context(nc.psum_tensor(f"ps_s{b}", [128, 1024], F32)) for b in range(2)]
            ps_t = st.enter_context(nc.psum_tensor("ps_t", [128, 1024], F32))
            ps_o = [st.enter_context(nc.psum_tensor(f"ps_o{b}", [128, 512], F32)) for b in range(2)]
            m_in, mk_ok, kr_in, qr_in, vc_in, kv_out = [
                sem(n, st) for n in ("m_in", "mk_ok", "kr_in", "qr_in", "vc_in", "kv_out")]
            b_in = [sem("bias_in0", st), sem("bias_in1", st)]
            vt_mm, vh_ok, vr_ok, qh_ok, qs_ok, kh_ok, kl_ok = [
                sem(n, st) for n in ("vt_mm", "vh_ok", "vr_ok", "qh_ok", "qs_ok", "kh_ok", "kl_ok")]
            s_mm, mx_ok, nm_ok, p_exp, tot_ok, rr_ok, turn, turn_v, pn_ok, t_mm, pth_ok, ptl_ok, pv_mm, oh_ok, ol_ok = [
                sem(n, st) for n in ("s_mm", "mx_ok", "nm_ok", "p_exp", "tot_ok", "rr_ok", "turn", "turn_v", "pn_ok", "t_mm", "pth_ok",
                                 "ptl_ok", "pv_mm", "oh_ok", "ol_ok")]
            S0, NM0, EX0, T0, PTL0, PV0, OL0 = 20, 20, 2, 3, 1, 2, 2
            block = st.enter_context(nc.Block())
            V_CTX = 2048
            ROUNDS = ((0, 4), (4, 8), (8, 12), (12, 16), (18, 20))

            def unit(u):
                hh, n = u // 10 % 2, u % 10
                return (hh, n // 4, n % 4) if n < 8 else (hh, None, n - 8)

            def blocked(ap):
                return ap.rearrange("p (j r c) -> p r j c", j=4, c=16)

            def backwards(ap):
                (ps, pn), (sa, na), (sb_, nb) = ap.ap
                return bass.AP(ap.tensor, ap.offset + (na - 1) * sa + (nb - 1) * sb_, [[ps, pn], [-sa, na], [-sb_, nb]])

            def slot(u):
                return u % U % 3

            def grid(ap, r0, rows, c0, cols):
                return ap.rearrange("p (r c) -> p r c", c=GW)[:, r0:r0 + rows, c0:c0 + cols]

            @block.sync
            def _(sp):
                def load_v(pair):
                    for b in range(4):
                        sp.dma_start(kr[:, 512 * b:512 * b + 512].rearrange("p (r c) -> p r c", c=32),
                                     grid(qkv_d[pair + 16, :, 0:LS], 0, 16, BANDS[b], 32)).then_inc(kr_in, 16)
                    sp.dma_start(kr[:, V_CTX:V_CTX + 256], qkv_d[pair + 16, :, LS:TOK]).then_inc(kr_in, 16)

                def load_q(pair, hh):
                    for half in range(2):
                        sp.dma_start(qr[64 * half:64 * half + 64, :],
                                     qkv_d[pair, 64 * hh:64 * hh + 64, :]).then_inc(qr_in, 16)

                def load_bias(pair, hh):
                    for r in range(8):
                        table = t["rpb"][pair * 2 + hh, :]
                        src = bass.AP(table.tensor, table.offset + ((r + 1) * RPB_W - 15), [[1, 16], [1, 16 * RPB_W]])
                        sp.dma_start(bias[16 * r:16 * r + 16, hh, :, :].rearrange("p a b -> p (a b)"),
                                     src).then_inc(b_in[hh], 16)

                def load_k(pair, hh):
                    for half in range(2):
                        rows = slice(64 * half, 64 * half + 64)
                        k = qkv_d[pair + 8, 64 * hh:64 * hh + 64, :]
                        sp.dma_start(kr[rows, 0:LS], k[:, 0:LS]).then_inc(kr_in, 16)
                        sp.dma_start(kr[rows, LS + 256:1536], k[:, LS:TOK]).then_inc(kr_in, 16)
                        sp.dma_start(kr[rows, LS:LS + 256], t["cache_kt"][pair * 2 + hh, :, :]).then_inc(kr_in, 16)

                load_q(0, 0)
                load_k(0, 0)
                flat = t["mask"].rearrange("p a b -> p (a b)")
                for n in range(2):
                    if n:
                        sp.wait_ge(mk_ok, 2)
                    sp.dma_start(pb[:, :, :].rearrange("p a b -> p (a b)")[:, 0:1152],
                                 flat[:, 1152 * n:1152 * n + 1152]).then_inc(m_in, 16)
                load_bias(0, 0)
                sp.wait_ge(kl_ok, 1)
                load_v(0)
                for n, name in ((1, "nk"), (2, "nv")):
                    sp.dma_start(t[name], qkv_d[8 * n:8 * n + 8, :, LS:TOK]).then_inc(kv_out, 16)

                def pair(i, following):
                    sp.wait_ge(kl_ok, i * 2 + 1)
                    sp.dma_start(vc[:, :, :], t["cache_v"][i, :, :, :]).then_inc(vc_in, 16)
                    sp.wait_ge(qs_ok, i * 2 + 1)
                    load_q(i, 1)
                    sp.wait_ge(nm_ok, i * 20 + 18)
                    load_bias(i, 1)
                    sp.wait_ge(vr_ok, i * 6 + 6)
                    load_k(i, 1)
                    sp.wait_ge(qs_ok, i * 2 + 2)
                    load_q(following, 0)
                    sp.wait_ge(kl_ok, i * 2 + 2)
                    load_k(following, 0)
                    sp.wait_ge(nm_ok, i * 20 + 28)
                    load_bias(following, 0)

                with sp.Fori(0, 7) as i:
                    pair(i, i + 1)
                    sp.wait_ge(kl_ok, i * 2 + 3)
                    load_v(i + 1)
                pair(7, 0)
                sp.wait_ge(kv_out, 32)

            def out_view(a, i, u):
                hh, half, j = unit(u)
                rows = slice(64 * hh, 64 * hh + 64)
                if half is None:
                    return rows, a[rows, i, LS + 128 * j:LS + 128 * j + 128]
                return rows, grid(a[rows, i, 0:LS], 8 * half, 8, 16 * j, 16)

            def src_view(rows, u):
                src = ps_o[u % 2][rows, 0:128]
                return src if unit(u)[1] is None else src.rearrange("p (r c) -> p r c", c=16)

            def run(eng, head, scores, values, steps):
                for n in range(4):
                    head(None, 0, n)
                scores(None, 0)
                scores(None, 1)
                with eng.Fori(0, 8) as i:
                    values(i)
                    for u in range(U + 1):
                        if 3 <= u < 7:
                            head(i, 1, u - 3)
                        if 13 <= u < 17:
                            head(i, 2, u - 13)
                        steps(i, u)

            def at_unit(i, c):
                return c if i is None else i * U + c

            def at_head(i, c, n=1):
                return c if i is None else i * (2 * n) + c

            @block.tensor
            def _(pe):
                pe.sem_inc(s_mm, S0)
                pe.sem_inc(t_mm, T0)
                pe.sem_inc(pv_mm, PV0)

                def values(i):
                    pe.wait_ge(kr_in, i * 272 + 176)
                    for r, (b0, b1) in enumerate(ROUNDS):
                        if r < 2:
                            pe.wait_ge(ptl_ok, i * U + PTL0)
                        else:
                            pe.wait_ge(vr_ok, i * 6 + (r - 1))
                        for b in range(b0, b1):
                            v0 = 128 * b if b < 16 else V_CTX + 128 * (b - 18)
                            src = kr[:, v0:v0 + 128]
                            o = (r % 2) * 512 + (b - b0) * 128
                            last = pe.transpose(ps_t[:, o:o + 128], src, ident[:, :])
                        last.then_inc(vt_mm, 1)

                def scores(i, u):
                    if i is None and u == 0:
                        pe.wait_ge(mk_ok, 3)
                    hh, half, j = unit(u)
                    if u % 10 == 0:
                        pe.wait_ge(qs_ok, at_head(i, u // 10 + 1))
                        pe.wait_ge(kl_ok, at_head(i, u // 10 + 1))
                    pe.wait_ge(p_exp, at_unit(i, EX0 + u - 1))
                    out = ps_s[u % 2]
                    if half is None:
                        q = qh[:, hh, LS + 128 * j:LS + 128 * j + 128]
                        for n, k in enumerate((kh, kl)):
                            last = pe.matmul(out[:, 512:768], q, k[:, hh, LS + 256:1536], start=n == 0, stop=n == 1)
                    else:
                        q = qh[:, hh, 256 * j + 128 * half:256 * j + 128 * half + 128]
                        loc = out[:, 0:384].rearrange("p (r c) -> p r c", c=32)
                        pe.matmul(out[:, 0:384], ident_b[:, :], mask[:, 3 * half + BIAS_T[j], :], start=True, stop=False)
                        for n, k in enumerate((kh, kl)):
                            pe.matmul(loc, q, grid(k[:, hh, 0:LS], 4 * half, 12, BANDS[j], 32), start=False, stop=n == 1)
                        for n, k in enumerate((kh, kl)):
                            last = pe.matmul(out[:, 512:768], q, k[:, hh, LS:LS + 256], start=n == 0, stop=n == 1)
                    last.then_inc(s_mm, 1)

                def blocks(u):
                    hh, half, j = unit(u)
                    if half is None:
                        return [(3, 18), (4, 19)]
                    return [(b, 4 * j + half + b) for b in range(3)] + [(3, 16), (4, 17)]

                def steps(i, u):
                    if u < U:
                        scores(i, u + 2)
                        if u == 0:
                            pe.wait_ge(vr_ok, i * 6 + 6)
                        pe.wait_ge(pn_ok, i * U + (u + 1))
                        pe.wait_ge(ptl_ok, i * U + (PTL0 + u))
                        for b, _ in blocks(u):
                            last = pe.transpose(ps_t[:, 128 * b:128 * b + 128], pb[:, slot(u), 128 * b:128 * b + 128],
                                                ident[:, :])
                        last.then_inc(t_mm, 1)
                    if u >= 1:
                        v = u - 1
                        pe.wait_ge(ptl_ok, i * U + (PTL0 + v + 1))
                        pe.wait_ge(ol_ok, i * U + (OL0 + v - 1))
                        prods = [(vt, b, vw, px) for b, vt in blocks(v)
                                 for vw, px in ((vh, pth), (vh, ptl), (vl, pth))]
                        for n, (vt, b, vw, px) in enumerate(prods):
                            last = pe.matmul(ps_o[v % 2][:, 0:128], vw[:, vt, :], px[:, v % 2, b, :],
                                             start=n == 0, stop=n == len(prods) - 1)
                        last.then_inc(pv_mm, 1)
                run(pe, lambda i, h, n: None, scores, values, steps)

            @block.scalar
            def _(act):
                act.sem_inc(p_exp, EX0)
                act.activation(ident_b[:, :], ident[:, :], ACT.Copy).then_inc(mk_ok, 1)
                for n in range(2):
                    act.wait_ge(m_in, 16 * n + 16)
                    act.activation(mask[:, :, :].rearrange("p a b -> p (a b)")[:, 1152 * n:1152 * n + 1152],
                                   pb[:, :, :].rearrange("p a b -> p (a b)")[:, 0:1152], ACT.Copy).then_inc(mk_ok, 1)

                def values(i):
                    act.wait_ge(pv_mm, i * U + PV0)
                    for r, (b0, b1) in enumerate(ROUNDS):
                        act.wait_ge(vt_mm, i * 5 + (r + 1))
                        o = (r % 2) * 512
                        act.activation(vh[:, b0:b1, :], ps_t[:, o:o + 128 * (b1 - b0)].rearrange(
                            "p (b n) -> p b n", n=128), ACT.Copy).then_inc(vh_ok, 1)
                    act.wait_ge(vc_in, i * 16 + 16)
                    act.activation(vh[:, 16:18, :], vc[:, :, :], ACT.Copy).then_inc(vh_ok, 1)

                def head(i, h, n):
                    hh = h % 2
                    if n == 0:
                        act.wait_ge(s_mm, at_unit(i, 10 * h + 10))
                        act.wait_ge(qr_in, at_head(i, 32 * h + 32, 32))
                        act.activation(blocked(qh[:, hh, 0:LS]), qr[:, 0:LS].rearrange("p (r j c) -> p r j c", j=4, c=16),
                                       ACT.Copy, scale=HD ** -0.5)
                        act.activation(qh[:, hh, LS:TOK], qr[:, LS:TOK], ACT.Copy, scale=HD ** -0.5).then_inc(qh_ok, 1)
                    else:
                        if n == 1:
                            act.wait_ge(kr_in, 96 if i is None else i * 272 + (96 * h + 176))
                        c = slice(512 * n - 512, 512 * n)
                        act.activation(kh[:, hh, c], kr[:, c], ACT.Copy).then_inc(kh_ok, 1)

                def exps(i, u):
                    _, half, _ = unit(u)
                    p, q = pb[:, slot(u), :], stat[:, u % 4, :]
                    act.wait_ge(nm_ok, at_unit(i, NM0 + u + 1))
                    if half is not None:
                        act.activation(p[:, 0:384], p[:, 0:384], ACT.Exp, bias=q[:, 2:3], accum_out=q[:, 3:4])
                    act.activation(p[:, 384:640], ps_s[u % 2][:, 512:768], ACT.Exp, bias=q[:, 2:3],
                                   accum_out=q[:, 4:5]).then_inc(p_exp, 1)

                def steps(i, u):
                    if u < U:
                        c0 = 0 if unit(u)[1] is not None else 3
                        act.wait_ge(t_mm, i * U + (T0 + u + 1))
                        act.wait_ge(pv_mm, i * U + (PV0 + u - 1))
                        act.activation(pth[:, u % 2, c0:5, :], ps_t[:, 128 * c0:640].rearrange(
                            "p (b n) -> p b n", n=128), ACT.Copy).then_inc(pth_ok, 1)
                        exps(i, u + 2)
                    if u >= 1:
                        act.wait_ge(pv_mm, i * U + (PV0 + u))
                        rows, dst = out_view(a_h, i, u - 1)
                        act.activation(dst, src_view(rows, u - 1), ACT.Copy).then_inc(oh_ok, 1)
                run(act, head, exps, values, steps)

            @block.gpsimd
            def _(pool):
                def head(i, h, n):
                    if n:
                        c = slice(512 * n - 512, 512 * n)
                        pool.wait_ge(kh_ok, at_head(i, 3 * h + n, 3))
                        ins = pool.tensor_tensor(kl[:, h % 2, c], kr[:, c], kh[:, h % 2, c].bitcast(F32), ALU.subtract)
                        if n == 3:
                            ins.then_inc(kl_ok, 1)

                def norm(i, u):
                    c0 = 0 if unit(u)[1] is not None else 384
                    pool.wait_ge(rr_ok, at_unit(i, u + 1))
                    pool.sem_inc(turn, 1)
                    pool.tensor_scalar(pb[:, slot(u), c0:640], pb[:, slot(u), c0:640], stat[:, u % 4, 6:7], 1.0,
                                       ALU.mult, ALU.mult).then_inc(pn_ok, 1)

                run(pool, head, lambda i, u: norm(i, 0) if u else None, lambda i: None,
                    lambda i, u: norm(i, u + 1) if u < U else None)

            @block.vector
            def _(dve):
                dve.sem_inc(nm_ok, NM0)
                dve.sem_inc(ptl_ok, PTL0)
                dve.sem_inc(ol_ok, OL0)

                def values(i):
                    for r, (b0, b1) in enumerate(ROUNDS):
                        dve.wait_ge(vh_ok, i * 6 + (r + 1))
                        o = (r % 2) * 512
                        dve.tensor_tensor(vl[:, b0:b1, :], ps_t[:, o:o + 128 * (b1 - b0)].rearrange(
                            "p (b n) -> p b n", n=128), vh[:, b0:b1, :].bitcast(F32), ALU.subtract).then_inc(vr_ok, 1)
                    dve.wait_ge(vh_ok, i * 6 + 6)
                    dve.tensor_tensor(vl[:, 16:18, :], vc[:, :, :],
                                      vh[:, 16:18, :].bitcast(F32), ALU.subtract).then_inc(vr_ok, 1)

                def head(i, h, n):
                    if n != 1:
                        return
                    dve.wait_ge(qh_ok, at_head(i, h + 1))
                    lo = qh[64:128, h % 2, :]
                    for j in range(4):
                        b = lo[:, 256 * j:256 * j + 256].rearrange("p (r c) -> p r c", c=16)
                        dve.scalar_tensor_tensor(b, grid(qr[64:128, 0:LS], 0, 16, 16 * j, 16), HD ** -0.5, b.bitcast(F32),
                                                 ALU.mult, ALU.subtract)
                    dve.scalar_tensor_tensor(lo[:, LS:TOK], qr[64:128, LS:TOK], HD ** -0.5, lo[:, LS:TOK].bitcast(F32),
                                             ALU.mult, ALU.subtract).then_inc(qs_ok, 1)

                def maxima(i, u):
                    hh, half, j = unit(u)
                    q, out = stat[:, u % 4, :], ps_s[u % 2]
                    dve.wait_ge(s_mm, at_unit(i, S0 + u + 1))
                    if i is not None:
                        last = u - 2 if u >= U else u - 3
                        dve.wait_ge(t_mm, i * U + (T0 + last + 1))
                    if half is not None:
                        if u % 10 == 0:
                            dve.wait_ge(b_in[hh], 128 if i is None else i * 128 + (128 * (u // 20) + 128))
                        x = BIAS_X[j]
                        dve.sem_inc(turn_v, 1)
                        dve.tensor_tensor_reduce(
                            out=pb[:, slot(u), 0:384].rearrange("p (r c) -> p r c", c=32),
                            in0=out[:, 0:384].rearrange("p (r c) -> p r c", c=32),
                            in1=backwards(bias[:, hh, 4 * half:4 * half + 12, 31 - x:63 - x]), scale=1.0, scalar=-3.0e38,
                            op0=ALU.add, op1=ALU.max, accum_out=q[:, 0:1])
                    dve.reduce_max(q[:, 1:2], out[:, 512:768], AX.X).then_inc(mx_ok, 1)
                    if u:
                        total(i, u - 1)
                    dve.wait_ge(mx_ok, at_unit(i, u + 1))
                    if half is not None:
                        ins = dve.tensor_scalar(q[:, 2:3], q[:, 0:1], q[:, 1:2], -1.0, ALU.max, ALU.mult)
                    else:
                        ins = dve.tensor_scalar(q[:, 2:3], q[:, 1:2], -1.0, None, ALU.mult)
                    ins.then_inc(nm_ok, 1)

                def total(i, u):
                    q = stat[:, u % 4, :]
                    dve.wait_ge(p_exp, at_unit(i, EX0 + u + 1))
                    if unit(u)[1] is not None:
                        dve.tensor_tensor(q[:, 5:6], q[:, 3:4], q[:, 4:5], ALU.add).then_inc(tot_ok, 1)
                    else:
                        dve.tensor_copy(q[:, 5:6], q[:, 4:5]).then_inc(tot_ok, 1)

                def recip(i, u):
                    q = stat[:, u % 4, :]
                    dve.wait_ge(tot_ok, at_unit(i, u + 1))
                    dve.reciprocal(q[:, 6:7], q[:, 5:6]).then_inc(rr_ok, 1)

                def softmax(i, u):
                    maxima(i, u)
                    if u:
                        recip(i, u - 1)

                def steps(i, u):
                    if u < U:
                        maxima(i, u + 2)
                        recip(i, u + 1)
                        c0 = 0 if unit(u)[1] is not None else 3
                        dve.wait_ge(pth_ok, i * U + (u + 1))
                        dve.tensor_tensor(ptl[:, u % 2, c0:5, :], ps_t[:, 128 * c0:640].rearrange(
                            "p (b n) -> p b n", n=128), pth[:, u % 2, c0:5, :].bitcast(F32),
                            ALU.subtract).then_inc(ptl_ok, 1)
                    if u >= 1:
                        dve.wait_ge(oh_ok, i * U + u)
                        rows, dst = out_view(a_l, i, u - 1)
                        hi = out_view(a_h, i, u - 1)[1]
                        dve.tensor_tensor(dst, src_view(rows, u - 1), hi.bitcast(F32), ALU.subtract).then_inc(ol_ok, 1)
                run(dve, head, softmax, values, steps)

        e0 = layer_rest(1, e0)
        assert e0 - wsh == t["w_all"].shape[0], (e0 - wsh, t["w_all"].shape)


def host_layout(inputs):
    f = np.float32
    g = {k: np.asarray(v) for k, v in inputs.items()}
    out = {}

    def cols(v):
        return v.reshape(-1, 128).T

    def entry(w):
        return w.reshape(-1, 128, 128).transpose(1, 0, 2).reshape(128, -1)

    def basis(b):
        e = np.zeros((128, 1024), f)
        x = entry(b.astype(f))
        e[:, :x.shape[1]] = x
        return e

    out["x"] = np.concatenate([g["x_sample"][0], g["x_prompt"][0]], 0).T.reshape(KT, 128, TOK)
    out["cvec"] = np.stack([g["c"][0], g["c_ctx"]], -1).reshape(8, 128, 2).transpose(1, 0, 2)
    conv = np.concatenate([g["hy_sconv_w"][0], g["hy_sconv_b"]], 0).reshape(4, 3, 8, 128)[:, [1, 2, 0]]
    conv = conv.transpose(3, 2, 1, 0).reshape(128, 96)
    ln = np.stack([g[n][l] for l in range(2) for n in ("ln1_g", "ln1_b", "ln2_g", "ln2_b")]).reshape(8, 8, 128)
    out["par"] = np.concatenate([conv, ln.transpose(2, 0, 1).reshape(128, 64), cols(g["hy_bias"][0]),
                                 cols(g["ada_b"].reshape(-1))], 1)
    out["ident"] = np.eye(128, dtype=f)
    out["ada"] = g["ada_w"][0].reshape(8, 128, 48, 128).transpose(2, 1, 0, 3).reshape(48, 128, 1024)
    out["ada_g"] = g["ada_w"].transpose(1, 0, 2).reshape(8, 128, 24, 512)[:, :, 10:].transpose(2, 1, 0, 3).reshape(14, 128, 4096)
    out["pe_w1"], out["pe_w2"] = g["hy_pe_w1"][0], g["hy_pe_w2"][0]
    out["fcol"] = np.stack([g["hy_pe_b1"][0], g["hy_pe_b2"][0], g["hy_sin_freq"][0, 0], g["hy_sin_freq"][0, 1]], 1)
    out["pe_w3"] = g["hy_pe_w3"][0].reshape(FILT, 2, 2, 512).transpose(2, 0, 1, 3)
    out["dec"] = np.broadcast_to(g["hy_decay"][0].reshape(2, 2, 512).transpose(1, 0, 2)[:, None], (2, 128, 2, 512))
    feats, negt = [], []
    for n in (LS, LP):
        order = np.concatenate([np.arange(0, n, 2), np.arange(1, n, 2)])
        tt = np.linspace(0.0, 1.0, n, dtype=f)[:, None]
        w = (f(2.0 * math.pi / n) * np.arange(n, dtype=f))[:, None]
        bands = np.linspace(1e-4, 15, 16, dtype=f)[None, :]
        feats.append(np.concatenate([tt, np.cos(bands * w), np.sin(bands * w)], -1)[order].T)
        negt.append(cols(-tt[order, 0]))
    out["feats"], out["negt"] = np.concatenate(feats, 1), np.concatenate(negt, 1)

    a_tiles = [np.arange(0, 256, 2), np.arange(1, 256, 2), np.arange(256, 512, 2), np.arange(257, 512, 2)]
    freq = a_tiles + [LS - 1 - a_tiles[a ^ 1] for a in range(4)]
    freq_p = [np.arange(128), LP - 1 - np.arange(128)]

    def angle(n, m, length):
        return np.outer(n, np.pi * (2 * m + 1) / (2 * length))

    filt = []
    for a in range(4):
        for fn in (np.cos, np.sin):
            n = np.concatenate([np.arange(0, LS, 2), np.arange(1, LS, 2)])
            filt.append(basis(fn(angle(n, freq[a], LS))))
    for fn in (np.cos, np.sin):
        n = np.concatenate([np.arange(0, LP, 2), np.arange(1, LP, 2)])
        filt.append(basis(fn(angle(n, freq_p[0], LP))))
    fwd = []
    for m in freq:
        x = angle(np.arange(LS // 2) + 0.5, m, LS)
        fwd.append(basis(np.concatenate([np.cos(x) + np.sin(x), np.cos(x) - np.sin(x)])))
    blocks = []
    for m in freq_p:
        x = angle(np.arange(LP // 2) + 0.5, m, LP)
        cas, cms, even = np.cos(x) + np.sin(x), np.cos(x) - np.sin(x), (m % 2 == 0)[None]
        blocks += [cas * even, cas * ~even, cms * ~even, cms * even]
    fwd.append(basis(np.concatenate(blocks)))
    inv = []
    for m in freq:
        x = angle(np.arange(LS // 2) + 0.5, m, LS).T
        inv += [np.cos(x) + np.sin(x), np.cos(x) - np.sin(x)]
    out["inv"] = (np.stack(inv, 1) / (2 * LS)).astype(f).reshape(128, 4, 2048).transpose(1, 0, 2)
    inv = []
    for m in freq_p:
        x = angle(np.arange(LP) + 0.5, m, LP).T
        inv += [np.cos(x) + np.sin(x), np.cos(x) - np.sin(x)]
    out["inv_p"] = (np.stack(inv, 1) / (2 * LP)).astype(f).reshape(128, 1024)

    def tiles(w):
        return w.reshape(8, 128, -1, 128).transpose(2, 1, 0, 3).reshape(-1, 128, 1024)

    w_in = tiles(g["hy_w_in"][0]).reshape(3, 8, 128, 1024)[[1, 2, 0]].transpose(1, 0, 2, 3).reshape(24, 128, 1024)

    def ffn(l):
        inn = tiles(g["ffn_w_in"][l]).reshape(2, FC, 2, 128, 1024).transpose(1, 2, 0, 3, 4).reshape(FC, 4, 128, 1024)
        o = g["ffn_w_out"][l].reshape(FC, 2, 128, 2, 4, 128).transpose(0, 3, 2, 4, 1, 5).reshape(FC, 2, 128, 1024)
        seq = [inn[0]]
        for i in range(1, FC):
            seq += [inn[i], o[i - 1]]
        return np.concatenate(seq + [o[FC - 1]])

    out["w_all"] = np.concatenate([np.stack(filt), np.stack(filt), w_in, np.stack(fwd), tiles(g["hy_w_out"][0]), ffn(0),
                                   tiles(g["na_w_qkv"][0]), tiles(g["na_w_out"][0]), ffn(1)])
    ck = g["cache_k"][0, 0]
    out["cache_kt"] = ck.transpose(0, 2, 1)
    out["cache_v"] = g["cache_v"][0, 0].reshape(8, 2, 2, 128, 64).transpose(0, 3, 2, 1, 4).reshape(8, 128, 2, 128)
    rpb = np.zeros((NH, RPB_H * RPB_W + RPB_W), f)
    rpb[:, :RPB_H * RPB_W].reshape(NH, RPB_H, RPB_W)[:, 4:19, 16:47] = g["na_rpb"][0]
    out["rpb"] = rpb[:, ::-1]
    mask = np.zeros((2, 3, 8, 16, 12, 32), f)
    for half in range(2):
        for j in (0, 1, 3):
            for r in range(8):
                row0 = min(max(8 * half + r - 4, 0), 8) - 4 * half
                for c in range(16):
                    col0 = min(max(16 * j + c - 8, 0), 48) - BANDS[j]
                    m = np.full((12, 32), MASKED, f)
                    m[row0:row0 + 8, col0:col0 + 16] = 0
                    mask[half, BIAS_T[j], r, c] = m
    out["mask"] = mask.reshape(2, 3, 128, 384).transpose(2, 0, 1, 3).reshape(128, 6, 384)
    return {k: np.ascontiguousarray(v, dtype=f) for k, v in out.items()}


def kernel(**inputs):
    import concourse.bacc as bacc
    from concourse.bass_utils import run_bass_kernel_spmd
    nc = bacc.Bacc("TRN2", target_bir_lowering=False, num_devices=1)
    arrays = host_layout(inputs)
    t = {k: nc.dram_tensor("in_" + k, v.shape, F32, kind="ExternalInput").ap() for k, v in arrays.items()}
    outs = {"y": (KT, 128, TOK), "nk": (8, 128, LP), "nv": (8, 128, LP)}
    for k, s in outs.items():
        t[k] = nc.dram_tensor("out_" + k, s, F32, kind="ExternalOutput").ap()
    hyena_natten_step(nc, t)
    r = run_bass_kernel_spmd(nc, [{"in_" + k: v for k, v in arrays.items()}], core_ids=[0]).results[0]
    y = r["out_y"].reshape(D, TOK).T
    kv = [r[n].reshape(1, 1, NH, HD, LP).transpose(0, 1, 2, 4, 3) for n in ("out_nk", "out_nv")]
    return (np.ascontiguousarray(y[LS:][None]), np.ascontiguousarray(y[:LS][None]),
            np.ascontiguousarray(kv[0]), np.ascontiguousarray(kv[1]))
```
